# Optimizing a Trainium2 kernel written in Bass

```python
import jax
import jax.numpy as jnp
from jax import lax
import numpy as np

D_MODEL = 1024
BATCH = 1
SEQ = 1024
DEPTH = 2

N_HEADS_A = 8
HEAD_DIM_A = 64
ROT_DIM = HEAD_DIM_A // 4
ROPE_THETA = 500000.0
DILATED_BRANCHES = ((128, 1), (512, 4), (2048, 16))
N_HEADS_B = 4
DV_B = 128
DK_B = DV_B // 2
GATE_RANK = 16
GATE_TAU = 16.0
GLA_CHUNK = 64
D_SGU = D_MODEL
N_GROUPS_C = 8
GROUP_C = D_SGU // N_GROUPS_C
SGU_CHUNK = 128
D_FF = 2816
CONV_W = 3

A_WIDTH = N_HEADS_A * HEAD_DIM_A
B_QK = N_HEADS_B * DK_B
B_V = N_HEADS_B * DV_B
AB_SPLITS = (A_WIDTH, A_WIDTH, A_WIDTH, B_QK, B_QK, B_V, B_V, GATE_RANK)
W_IN_AB = 3 * A_WIDTH + 2 * B_QK + 2 * B_V + GATE_RANK
NEG = -1e30
EPS = 1e-6

kernel_name = 'hybrid_dilated_gla_sgu_convffn'

def rms_norm(x, g):
    xf = x.astype(jnp.float32)
    y = xf * lax.rsqrt(jnp.mean(xf * xf, axis=-1, keepdims=True) + EPS)
    return (y * g.astype(jnp.float32)).astype(x.dtype)

def split_heads(t, n):
    b, s, _ = t.shape
    return t.reshape(b, s, n, -1).transpose(0, 2, 1, 3)

def merge_heads(t):
    b, h, s, d = t.shape
    return t.transpose(0, 2, 1, 3).reshape(b, s, h * d)

def partial_rope(x, positions):
    half = ROT_DIM // 2
    inv = ROPE_THETA ** (-jnp.arange(half, dtype=jnp.float32) * (2.0 / ROT_DIM))
    ang = positions.astype(jnp.float32)[:, None, :, None] * inv
    cos, sin = jnp.cos(ang), jnp.sin(ang)
    xr = x[..., :ROT_DIM].astype(jnp.float32)
    x1, x2 = xr[..., :half], xr[..., half:]
    rot = jnp.concatenate([x1 * cos - x2 * sin, x2 * cos + x1 * sin], axis=-1)
    return jnp.concatenate([rot.astype(x.dtype), x[..., ROT_DIM:]], axis=-1)

def dilated_branch(q, k, v, window, dilation):
    B, H, S, Dh = q.shape
    blk = window // dilation
    span = blk * dilation
    Sp = -(-S // span) * span
    nb = Sp // span

    def to_blocks(t):
        t = jnp.pad(t, ((0, 0), (0, 0), (0, Sp - S), (0, 0)))
        t = t.reshape(B, H, nb * blk, dilation, Dh).transpose(0, 1, 3, 2, 4)
        return t.reshape(B, H, dilation, nb, blk, Dh)

    def with_prev(t):
        prev = jnp.pad(t, ((0, 0), (0, 0), (0, 0), (1, 0), (0, 0), (0, 0)))[:, :, :, :-1]
        return jnp.concatenate([prev, t], axis=4)

    qb = to_blocks(q)
    kk = with_prev(to_blocks(k))
    vv = with_prev(to_blocks(v))
    s = jnp.einsum('bhrnqd,bhrnkd->bhrnqk', qb, kk,
                   preferred_element_type=jnp.float32) * (Dh ** -0.5)
    a = jnp.arange(blk)[:, None]
    c = jnp.arange(2 * blk)[None, :]
    band = (c >= a) & (c <= a + blk)
    valid_prev = (jnp.arange(nb)[:, None, None] > 0) | (c[None] >= blk)
    mask = band[None] & valid_prev
    s = jnp.where(mask, s, NEG)
    m = jnp.max(s, axis=-1)
    p = jnp.exp(s - m[..., None])
    l = jnp.sum(p, axis=-1)
    o = jnp.einsum('bhrnqk,bhrnkd->bhrnqd', p.astype(vv.dtype), vv,
                   preferred_element_type=jnp.float32) / l[..., None]

    def from_blocks(t):
        x_ = t.shape[-1]
        t = t.reshape(B, H, dilation, nb * blk, x_).transpose(0, 1, 3, 2, 4)
        return t.reshape(B, H, Sp, x_)[:, :, :S]

    return from_blocks(o), from_blocks(m[..., None])[..., 0], from_blocks(l[..., None])[..., 0]

def dilated_attention(q, k, v):
    outs = [dilated_branch(q, k, v, w, d) for (w, d) in DILATED_BRANCHES]
    ms = jnp.stack([m for _, m, _ in outs])
    ls = jnp.stack([l for _, _, l in outs])
    os_ = jnp.stack([o for o, _, _ in outs])
    wts = ls * jnp.exp(ms - jnp.max(ms, axis=0, keepdims=True))
    o = jnp.einsum('gbhs,gbhsd->bhsd', wts, os_) / jnp.sum(wts, axis=0)[..., None]
    return o

def gla(q, k, v, log_a):
    B, H, S, DK = q.shape
    DV = v.shape[-1]
    C = GLA_CHUNK
    N = S // C
    f32 = jnp.float32
    q = q.astype(f32).reshape(B, H, N, C, DK) * (DK ** -0.5)
    k = k.astype(f32).reshape(B, H, N, C, DK)
    v = v.astype(f32).reshape(B, H, N, C, DV)
    b = jnp.cumsum(log_a.astype(f32).reshape(B, H, N, C, DK), axis=3)
    b_last = b[:, :, :, C - 1:C]
    b_ref = b[:, :, :, C // 2 - 1:C // 2]
    att = jnp.einsum('bhnik,bhnjk->bhnij', q * jnp.exp(b - b_ref), k * jnp.exp(b_ref - b))
    att = jnp.where(jnp.tril(jnp.ones((C, C), dtype=bool)), att, 0.0)
    o = jnp.einsum('bhnij,bhnjv->bhniv', att, v)
    chunk_kv = jnp.einsum('bhnjk,bhnjv->bhnkv', k * jnp.exp(b_last - b), v)
    decay = jnp.exp(b_last[:, :, :, 0])

    def step(state, inp):
        kv, dec = inp
        return state * dec[..., None] + kv, state

    _, states = lax.scan(step, jnp.zeros((B, H, DK, DV), f32),
                         (chunk_kv.transpose(2, 0, 1, 3, 4), decay.transpose(2, 0, 1, 3)))
    states = states.transpose(1, 2, 0, 3, 4)
    o = o + jnp.einsum('bhnik,bhnkv->bhniv', q * jnp.exp(b), states)
    return o.reshape(B, H, S, DV)

def mixer_ab(h, positions, w_in, w_gate_up, b_gate_up, g_out_b, w_out):
    z = h @ w_in
    offs = []
    acc = 0
    for size in AB_SPLITS[:-1]:
        acc += size
        offs.append(acc)
    qa, ka, va, qb, kb, vb, rb, gl = jnp.split(z, offs, axis=-1)
    qa = partial_rope(split_heads(qa, N_HEADS_A), positions)
    ka = partial_rope(split_heads(ka, N_HEADS_A), positions)
    oa = dilated_attention(qa, ka, split_heads(va, N_HEADS_A))
    g = (gl @ w_gate_up + b_gate_up).astype(jnp.float32)
    log_a = jax.nn.log_sigmoid(g) / GATE_TAU
    ob = gla(split_heads(qb, N_HEADS_B), split_heads(kb, N_HEADS_B),
             split_heads(vb, N_HEADS_B), split_heads(log_a, N_HEADS_B))
    ob = rms_norm(ob, g_out_b) * jax.nn.silu(split_heads(rb, N_HEADS_B).astype(jnp.float32))
    o = jnp.concatenate([merge_heads(oa), merge_heads(ob)], axis=-1).astype(h.dtype)
    return o @ w_out

def mixer_c(h, w_in_c, g_sgu, w_spatial, b_spatial, w_out_c):
    B, S, _ = h.shape
    z = jax.nn.gelu(h @ w_in_c)
    u, v = jnp.split(z, 2, axis=-1)
    v = rms_norm(v, g_sgu).reshape(B, S // SGU_CHUNK, SGU_CHUNK, N_GROUPS_C, GROUP_C)
    ws = w_spatial * jnp.tril(jnp.ones((SGU_CHUNK, SGU_CHUNK), dtype=w_spatial.dtype))
    sv = jnp.einsum('gts,bnsgc->bntgc', ws, v) + b_spatial.T[:, :, None]
    return (u * sv.reshape(B, S, D_SGU)) @ w_out_c

def conv_ffn(h, w_up, conv_w, conv_b, w_down):
    S = h.shape[1]
    z = h @ w_up
    zp = jnp.pad(z, ((0, 0), (CONV_W - 1, 0), (0, 0)))
    z = sum(zp[:, j:j + S] * conv_w[j] for j in range(CONV_W)) + conv_b
    gate, up = jnp.split(z, 2, axis=-1)
    return (jax.nn.silu(gate) * up) @ w_down

def setup_inputs(seed: int = 0) -> dict:
    key = jax.random.key(seed)
    ks = jax.random.split(key, 24)
    f32 = jnp.float32
    n_even = (DEPTH + 1) // 2
    n_odd = DEPTH // 2
    out_scale = (2 * DEPTH) ** -0.5

    def normal(k, shape, scale):
        return jax.random.normal(k, shape, f32) * scale

    def gain(k, shape):
        return 1.0 + 0.02 * jax.random.normal(k, shape, f32)

    x = normal(ks[0], (BATCH, SEQ, D_MODEL), 1.0)
    positions = (jnp.arange(SEQ, dtype=jnp.int32)[None, :]
                 + jax.random.randint(ks[1], (BATCH, 1), 0, 4096, dtype=jnp.int32))
    return {
        'x': x,
        'positions': positions,
        'norm_mix': gain(ks[2], (DEPTH, D_MODEL)),
        'norm_ffn': gain(ks[3], (DEPTH, D_MODEL)),
        'w_in_ab': normal(ks[4], (n_even, D_MODEL, W_IN_AB), D_MODEL ** -0.5),
        'w_gate_up': normal(ks[5], (n_even, GATE_RANK, B_QK), GATE_RANK ** -0.5),
        'b_gate_up': normal(ks[6], (n_even, B_QK), 0.1),
        'g_out_b': gain(ks[7], (n_even, DV_B)),
        'w_out_ab': normal(ks[8], (n_even, D_MODEL, D_MODEL), D_MODEL ** -0.5 * out_scale),
        'w_in_c': normal(ks[9], (n_odd, D_MODEL, 2 * D_SGU), D_MODEL ** -0.5),
        'g_sgu': gain(ks[10], (n_odd, D_SGU)),
        'w_spatial': normal(ks[11], (n_odd, N_GROUPS_C, SGU_CHUNK, SGU_CHUNK), SGU_CHUNK ** -0.5),
        'b_spatial': 1.0 + normal(ks[12], (n_odd, N_GROUPS_C, SGU_CHUNK), 0.05),
        'w_out_c': normal(ks[13], (n_odd, D_SGU, D_MODEL), D_SGU ** -0.5 * out_scale),
        'w_up': normal(ks[14], (DEPTH, D_MODEL, 2 * D_FF), D_MODEL ** -0.5),
        'conv_w': normal(ks[15], (DEPTH, CONV_W, 2 * D_FF), CONV_W ** -0.5),
        'conv_b': normal(ks[16], (DEPTH, 2 * D_FF), 0.01),
        'w_down': normal(ks[17], (DEPTH, D_FF, D_MODEL), D_FF ** -0.5 * out_scale),
        'norm_final': gain(ks[18], (D_MODEL,)),
    }

def reference(x, positions, norm_mix, norm_ffn, w_in_ab, w_gate_up, b_gate_up, g_out_b,
              w_out_ab, w_in_c, g_sgu, w_spatial, b_spatial, w_out_c, w_up, conv_w, conv_b,
              w_down, norm_final):
    h = x
    for layer in range(DEPTH):
        i = layer // 2
        hn = rms_norm(h, norm_mix[layer])
        if layer % 2 == 0:
            h = h + mixer_ab(hn, positions, w_in_ab[i], w_gate_up[i], b_gate_up[i],
                             g_out_b[i], w_out_ab[i])
        else:
            h = h + mixer_c(hn, w_in_c[i], g_sgu[i], w_spatial[i], b_spatial[i], w_out_c[i])
        h = h + conv_ffn(rms_norm(h, norm_ffn[layer]), w_up[layer], conv_w[layer],
                         conv_b[layer], w_down[layer])
    return rms_norm(h, norm_final)


_drawn_inputs = setup_inputs


def setup_inputs(seed=0):
    import zlib

    import numpy as np

    out = dict(_drawn_inputs(seed))
    spreads = {}
    factors = {'norm_mix': 4.26,
     'norm_ffn': 5.096,
     'b_gate_up': 5.397,
     'g_out_b': 8.0,
     'g_sgu': 8.0,
     'b_spatial': 3.925,
     'conv_b': 8.0,
     'norm_final': 2.896}
    for name, (base, spread) in spreads.items():
        noise = np.random.default_rng([zlib.crc32(name.encode()), seed]).standard_normal(out[name].shape)
        drawn = base * np.exp(spread * noise) if base else spread * noise
        out[name] = jnp.asarray(drawn.astype(out[name].dtype))
    for name, factor in factors.items():
        out[name] = (out[name] * factor).astype(out[name].dtype)
    return out
```

```python
from contextlib import ExitStack

import numpy as np

import concourse.bass as bass
from concourse import mybir

F32 = mybir.dt.float32
F32R = mybir.dt.float32r
I32 = mybir.dt.int32
U32 = mybir.dt.uint32
ALU = mybir.AluOpType
ACT = mybir.ActivationFunctionType

P = 128
D = 1024
S = 1024
HALF = 512
KT = D // P
ST = S // P
NHP = 4
NBP = 2
CH = 64
NCH = S // CH
FT = 2816 // P
NBLK = FT // 2
ROT = 16
THETA = 500000.0
EPS = 1e-6
A_SCALE = 0.125
TAU = 16.0
NEG = -1e30
BRANCHES = ((128, 1), (512, 4), (2048, 16))

QA, KA, VA, QB, KB, VB, RB = 0, 4, 8, 12, 14, 16, 20

C_ID, C_U, C_TRIL, C_M64, C_INV, C_SGN, C_N = 0, 128, 256, 384, 512, 513, 514
G_MIX0, G_MIX1, G_FFN0, G_FFN1, G_FIN, G_SGU, G_OUT, G_N = 0, 8, 16, 24, 32, 40, 48, 49

TWO_PI = 2.0 * np.pi
PI_PARTS = []
_rest = TWO_PI
for _k in range(3):
    _e = 2.0 ** (np.floor(np.log2(_rest)) - 7)
    _c = float(np.floor(_rest / _e) * _e)
    PI_PARTS.append(_c)
    _rest -= _c
PI_PARTS.append(float(np.float32(_rest)))
MAGIC = 12582912.0


def constant_arrays():
    c = np.zeros((P, C_N), np.float32)
    p = np.arange(P)
    c[:, C_ID:C_ID + P] = np.eye(P)
    same = (p[:, None] // CH) == (p[None, :] // CH)
    upper = p[:, None] <= p[None, :]
    c[:, C_U:C_U + P] = (same & upper) / TAU
    c[:, C_TRIL:C_TRIL + P] = upper
    c[:, C_M64:C_M64 + P] = same & upper
    half = ROT // 2
    r = p % 64
    inv = np.float32(THETA) ** (-np.arange(half, dtype=np.float32) * np.float32(2.0 / ROT))
    c[:, C_INV] = np.where(r < ROT, inv[r % half], 0.0)
    c[:, C_SGN] = np.where(r < half, -1.0, np.where(r < ROT, 1.0, 0.0))
    d = (ST - 1) * P + p[:, None] - np.arange(S)[None, :]
    count = np.zeros((P, S), np.float64)
    for window, dil in BRANCHES:
        count += (d >= 0) & (d <= window) & (d % dil == 0)
    m = np.where(count > 0, np.log(np.maximum(count, 1.0)) / A_SCALE, NEG)
    return c, m.astype(np.float32)


def build(nc, xT, pos, consts, logmul, gains, wgu, bgu, wgl, w_in, w_out, w_u, w_v, w_outc, wsT, bsp,
          w_up, w_dn, conv, outT):
    with ExitStack() as ctx:
        arena = -(-nc.sbuf_base // 64) * 64

        def sb(name, kb, shape, dt=F32):
            return nc.alloc_sbuf_tensor_at(name, shape, dt, offset=arena + int(kb * 1024))

        def sem(name):
            return ctx.enter_context(nc.semaphore(name))

        act_hi = sb("act_hi", 0, [P, KT, S], F32R)
        act_lo = sb("act_lo", 32, [P, KT, S], F32R)
        w_hi = sb("w_hi", 64, [P, 4, 1024], F32R)
        w_lo = sb("w_lo", 80, [P, 4, 1024], F32R)
        w_raw = sb("w_raw", 96, [P, 2, 1024])
        x = sb("x", 104, [P, KT, S])
        rstd = sb("rstd", 168, [P, S])
        sq = sb("sq", 172, [P, 2, S])
        acc = sb("acc", 180, [P, S])
        cst = sb("cst", 200, [P, C_N])
        gain = sb("gain", 202.25, [P, G_N])
        ones = sb("ones", 202.5, [P, P])
        cw = sb("cw", 203, [P, 2, 2 * FT, 4])
        tiny = sb("tiny", 204.5, [P, 64])
        carry = sb("carry", 204.75, [P, 4])
        g_hi = sb("g_hi", 136, [P, 4, S], F32R)
        g_lo = sb("g_lo", 152, [P, 4, S], F32R)
        fz = sb("fz", 184, [P, 2, S])
        fc = sb("fc", 192, [P, 2, S])
        oT = sb("oT", 136, [P, KT, S])
        vs = sb("vs", 136, [P, KT, ST, P])
        cz = sb("cz", 184, [P, 2, S])
        bspb = sb("bspb", 192, [P, KT * P])
        wst = sb("wst", 196, [P, KT, P])
        ropeC = sb("ropeC", 184, [P, S])
        ropeS = sb("ropeS", 188, [P, S])
        lmul = sb("lmul", 192, [P, S])
        glT = sb("glT", 196, [P, S])
        scr = [104 + 4 * i for i in range(8)]
        b_k, b_q = sb("b_k", scr[0], [P, S]), sb("b_q", scr[1], [P, S])
        b_cum, b_e = sb("b_cum", scr[2], [P, S]), sb("b_e", scr[3], [P, S])
        b_kd, b_qe = sb("b_kd", scr[4], [P, S]), sb("b_qe", scr[5], [P, S])
        b_vn = sb("b_vn", scr[6], [P, ST, 2 * P])
        b_la = sb("b_la", 72, [P, ST, P])
        b_kdn = sb("b_kdn", 76, [P, ST, P])
        b_r = sb("b_r", 88, [P, 2, S])
        b_vt = sb("b_vt", 136, [P, 2, S])
        b_st = sb("b_st", 144, [P, NCH, P])
        b_att = sb("b_att", 172, [P, S])
        b_v = sb("b_v", 180, [P, S])
        wgu_sb = sb("wgu_sb", 205, [P, 256])
        wgl_raw = sb("wgl_raw", 206, [P, KT * 16])
        wgl_hi = sb("wgl_hi", 206.5, [P, KT, 16], F32R)
        wgl_lo = sb("wgl_lo", 207, [P, KT, 16], F32R)
        a_vt = sb("a_vt", scr[0], [P, S])
        a_vn = sb("a_vn", scr[1], [P, ST, P])
        a_k, a_q = sb("a_k", scr[2], [P, S]), sb("a_q", scr[3], [P, S])
        a_sh, a_t = sb("a_sh", scr[4], [P, S]), sb("a_t", scr[5], [P, S])
        a_s = sb("a_s", scr[6], [P, 2, S])
        a_pt = sb("a_pt", 172, [P, 2, S])
        pos_i = sb("pos_i", 152, [P, S], I32)
        r_a, r_n, r_r = sb("r_a", 176, [P, S]), sb("r_n", 136, [P, S]), sb("r_r", 140, [P, S])

        ident = cst[:, C_ID:C_ID + P]
        ps = ctx.enter_context(nc.psum_tensor("ps", [P, 8, HALF], F32))

        def slot2(r):
            b = 2 * (r % 4)
            return ps[:, b:b + 2, :].rearrange("p b n -> p (b n)")

        s_cst = sem("constants_loaded")
        s_tab = sem("tables_loaded")
        s_wglr = sem("w_gl_loaded")
        s_cmx = sem("mixer_c_constants_loaded")
        s_x = [sem(f"x_loaded{k}") for k in range(KT)]
        s_wdma = [sem("w_loaded0"), sem("w_loaded1")]
        s_wsplit = sem("w_split")
        s_whi = sem("w_hi_done")
        s_proj = sem("projected")
        s_out = sem("out_stored")
        s_setup = sem("setup_done")

        class Norm:
            def __init__(self, name, col):
                self.col = col
                self.sq = sem(name + "_squared")
                self.acc = sem(name + "_accumulated")
                self.hi = sem(name + "_hi")
                self.lo = sem(name + "_lo")
                self.sum = sem(name + "_summed")
                self.var = sem(name + "_var")
                self.ln = sem(name + "_ln")
                self.exp = sem(name + "_exp")
                self.rstd = sem(name + "_rstd")

        norms = [Norm("norm_a", G_MIX0), Norm("norm_f0", G_FFN0), Norm("norm_c", G_MIX1),
                 Norm("norm_f1", G_FFN1), Norm("norm_out", G_FIN)]

        N_B = 0
        N_A = N_B + 6 * NBP
        N_WO = N_A + 3 * NHP
        N_F0 = N_WO + KT
        FFN_TILES = 3 * FT
        N_V = N_F0 + FFN_TILES
        N_CU = N_V + 8
        N_WOC = N_CU + KT
        N_F1 = N_WOC + KT

        s_wgl = sem("w_gl_split")
        s_fin = sem("final_tile")

        class Bsem:
            def __init__(self):
                self.ready = sem("b_result_ready")
                self.free = sem("b_result_taken")
                self.silu = sem("b_silu")
                self.gl = sem("b_gl_projected")
                self.min = sem("b_min")
                self.e = sem("b_exp_ln")
                self.la = sem("b_log_decay")
                self.dec = sem("b_vector_steps")
                self.state = sem("b_state")
                self.o = sem("b_out_steps")
                self.osq = sem("b_out_act")
        B = Bsem()

        class Asem:
            def __init__(self):
                self.ready = sem("a_v_transposed")
                self.free = sem("a_proj_taken")
                self.vn = sem("a_v_by_position")
                self.rope = sem("a_rope_steps")
                self.k = sem("a_k_ready")
                self.q = sem("a_q_ready")
                self.s = sem("a_scores_ready")
                self.max = sem("a_max_done")
                self.e = sem("a_exp_done")
                self.rl = sem("a_recip_done")
                self.p = sem("a_probs_ready")
                self.pt = sem("a_transposed")
                self.ptf = sem("a_transposed_taken")
                self.pv = sem("a_pv_done")
                self.of = sem("a_out_taken")
        A = Asem()

        class Osem:
            def __init__(self, name):
                self.hi = sem(name + "_hi")
                self.lo = sem(name + "_lo")
                self.added = sem(name + "_added")
        WO, WOC = Osem("wo"), Osem("woc")

        class Fsem:
            def __init__(self, name):
                self.free = sem(name + "_taken")
                self.tap = sem(name + "_taps")
                self.cid = sem(name + "_conv_start")
                self.silu = sem(name + "_silu")
                self.gated = sem(name + "_gated")
                self.ghi = sem(name + "_g_hi")
                self.glo = sem(name + "_g_lo")
        f0, f1 = Fsem("f0"), Fsem("f1")

        class Csem:
            def __init__(self):
                self.slot = sem("c_v_weight_slot_used")
                self.vf = sem("c_v_gelu")
                self.vsq = sem("c_v_squares")
                self.rn = sem("c_rstd_rows")
                self.rnf = sem("c_rstd_rows_taken")
                self.t = sem("c_tiny_steps")
                self.ta = sem("c_tiny_act")
                self.vn = sem("c_v_normed")
                self.ws = sem("c_spatial_masked")
                self.ready = sem("c_result_ready")
                self.free = sem("c_result_taken")
                self.u = sem("c_u_gelu")
                self.gated = sem("c_gated")
        C = Csem()
        s_rope_v = sem("rope_vector_steps")
        s_rope_a = sem("rope_scalar_steps")
        s_xr = sem("x_reloaded")

        R_A = 6 * NBP
        R_WO = R_A + 3 * NHP
        R_F0 = R_WO + KT
        FFN_RESULTS = 4 * NBLK + KT * NBLK
        R_V = R_F0 + FFN_RESULTS
        R_CU = R_V + 2 * ST
        R_WOC = R_CU + KT
        R_F1 = R_WOC + KT

        block = ctx.enter_context(nc.Block())

        @block.sync
        def _(sp):
            def plain(n, src):
                if n >= 2:
                    sp.wait_ge(s_wsplit, n - 1)
                sp.dma_start(w_raw[:, n % 2, :], src).then_inc(s_wdma[n % 2], 16)

            def looped(base, per, i, t, src):
                sp.wait_ge(s_wsplit, i * per + (base + t - 1))
                sp.dma_start(w_raw[:, (base + t) % 2, :], src).then_inc(s_wdma[(base + t) % 2], 16)

            sp.dma_start(cst[:], consts).then_inc(s_cst, 16)
            sp.dma_start(gain[:], gains).then_inc(s_cst, 16)
            sp.dma_start(cw[:], conv).then_inc(s_cst, 16)
            for k in range(KT):
                sp.dma_start(x[:, k, :], xT[k]).then_inc(s_x[k], 16)
                if k == 1:
                    sp.dma_start(wgl_raw[:], wgl).then_inc(s_wglr, 16)
            sp.dma_start(pos_i[:], pos.partition_broadcast(P)).then_inc(s_tab, 16)
            sp.dma_start(lmul[:], logmul).then_inc(s_tab, 16)
            sp.dma_start(wgu_sb[0:16, :], wgu).then_inc(s_tab, 16)
            sp.dma_start(wgu_sb[16:17, :], bgu).then_inc(s_tab, 16)

            for bp in range(NBP):
                for t, blk in enumerate((KB + bp, QB + bp, VB + 2 * bp, VB + 2 * bp + 1, RB + 2 * bp, RB + 2 * bp + 1)):
                    plain(N_B + 6 * bp + t, w_in[blk])
            for hp in range(NHP):
                for t, blk in enumerate((VA + hp, KA + hp, QA + hp)):
                    plain(N_A + 3 * hp + t, w_in[blk])
            for m in range(KT):
                plain(N_WO + m, w_out[m])

            def ffn(base, layer):
                for t in range(4):
                    plain(base + t, w_up[layer, t])
                with sp.Fori(0, NBLK - 1) as i:
                    for t in range(4):
                        looped(base + 4, 6, i, t, w_up[layer, bass.ds(i * 4 + (4 + t), 1)].rearrange("a p n -> p (a n)"))
                    for t in range(2):
                        looped(base + 4, 6, i, 4 + t, w_dn[layer, bass.ds(i * 2 + t, 1)].rearrange("a p n -> p (a n)"))
                for t in range(2):
                    plain(base + FFN_TILES - 2 + t, w_dn[layer, FT - 2 + t])

            ffn(N_F0, 0)
            for t in range(8):
                plain(N_V + t, w_v[t])
                if t == 0:
                    sp.wait_ge(f0.glo, FT)
                    sp.dma_start(bspb[:], bsp.partition_broadcast(P)).then_inc(s_cmx, 16)
                    sp.dma_start(wst[:], wsT).then_inc(s_cmx, 16)
            for m in range(KT):
                plain(N_CU + m, w_u[m])
            for m in range(KT):
                plain(N_WOC + m, w_outc[m])
            ffn(N_F1, 1)
            for k in range(KT):
                sp.wait_ge(s_fin, k + 1)
                sp.dma_start(outT[k], x[:, k, :]).then_inc(s_out, 16)
            sp.wait_ge(s_out, 16 * KT)

        @block.gpsimd
        def _(pool):
            def split(parity, loaded, slot, done, *free):
                pool.wait_ge(s_wdma[parity], loaded)
                for s_free, count in free:
                    pool.wait_ge(s_free, count)
                pool.tensor_tensor(tiny[:, 62:63], w_raw[:, parity, 0:1], w_raw[:, parity, 0:1], ALU.mult)
                pool.tensor_scalar(w_hi[:, slot, :], w_raw[:, parity, :], 1.0, None, ALU.mult).then_inc(s_whi, 1)
                pool.wait_ge(s_whi, done)
                pool.tensor_tensor(w_lo[:, slot, :], w_raw[:, parity, :], w_hi[:, slot, :].bitcast(F32),
                                   ALU.subtract).then_inc(s_wsplit, 1)

            def plain(n, slot, *free):
                split(n % 2, 16 * (n // 2 + 1), slot, n + 2, *free)

            def looped(n0, i, per, slot, *free):
                split(n0 % 2, i * (8 * per) + 16 * (n0 // 2 + 1), slot, i * per + (n0 + 2), *free)

            pool.wait_ge(s_wglr, 16)
            pool.tensor_scalar(wgl_hi[:], wgl_raw[:], 1.0, None, ALU.mult).then_inc(s_whi, 1)
            pool.wait_ge(s_whi, 1)
            pool.tensor_tensor(wgl_lo[:], wgl_raw[:], wgl_hi[:].bitcast(F32), ALU.subtract).then_inc(s_wgl, 1)
            plain(0, 0)
            plain(1, 1)
            with pool.Fori(0, (N_F0 - 2) // 2) as i:
                for t in range(2):
                    looped(2 + t, i, 2, t, (s_proj, i * 2 + (t + 1)))

            def ffn(base, res):
                for t in range(4):
                    plain(base + t, t, (s_proj, res - 1 if t == 0 else res))
                with pool.Fori(0, NBLK - 1) as i:
                    for t in range(4):
                        looped(base + 4 + t, i, 6, t % 2, (s_proj, i * 12 + (res + t + (1 if t < 2 else 3))))
                    for t in range(2):
                        looped(base + 8 + t, i, 6, 2 + t, (s_proj, i * 12 + (res + 4)))
                for t in range(2):
                    plain(base + FFN_TILES - 2 + t, 2 + t, (s_proj, res + FFN_RESULTS - KT))

            ffn(N_F0, R_F0)
            for t in range(4):
                plain(N_V + t, t, (s_proj, R_V - KT if t < 2 else R_V))
            for t in range(4):
                plain(N_V + 4 + t, t, (C.slot, t + 1) if t < 3 else (s_proj, R_V + ST))
            for m in range(KT):
                plain(N_CU + m, m % 2, (C.slot, 4 + m) if m < 2 else (s_proj, R_CU + m - 1))
            plain(N_WOC, 0, (s_proj, R_WOC - 1))
            plain(N_WOC + 1, 1, (s_proj, R_WOC))
            with pool.Fori(0, (KT - 2) // 2) as i:
                for t in range(2):
                    looped(N_WOC + 2 + t, i, 2, t, (s_proj, i * 2 + (R_WOC + t + 1)))
            ffn(N_F1, R_F1)

        def kv_col(c):
            return (c % 2) * HALF + (c // 2) * 256

        def groups_before(u):
            return sum(1 if v % 8 < 4 else 2 for v in range(u))

        @block.tensor
        def _(pe):
            def cross(out_of, act_hi_k, act_lo_k, wh, wl, k, first, last):
                out = out_of
                ins = None
                for h in range(2):
                    cols = slice(h * HALF, (h + 1) * HALF)
                    pe.matmul(out[:, cols], wh, act_hi_k[:, cols], start=first, stop=False)
                for h in range(2):
                    cols = slice(h * HALF, (h + 1) * HALF)
                    pe.matmul(out[:, cols], wh, act_lo_k[:, cols], start=False, stop=False)
                for h in range(2):
                    cols = slice(h * HALF, (h + 1) * HALF)
                    ins = pe.matmul(out[:, cols], wl, act_hi_k[:, cols], start=False, stop=last)
                return ins

            def project(out, slot, split_done, lo_sem=None):
                pe.wait_ge(s_wsplit, split_done)
                for k in range(KT):
                    if lo_sem is not None:
                        pe.wait_ge(lo_sem, k + 1)
                    ins = cross(out, act_hi[:, k, :], act_lo[:, k, :], w_hi[:, slot, k * P:(k + 1) * P],
                                w_lo[:, slot, k * P:(k + 1) * P], k, k == 0, k == KT - 1)
                ins.then_inc(s_proj, 1)

            def sum_squares(norm, out):
                pe.wait_ge(norm.acc, KT)
                for h in range(2):
                    ins = pe.matmul(out[:, h * HALF:(h + 1) * HALF], ones[:], acc[:, h * HALF:(h + 1) * HALF],
                                    start=True, stop=True)
                ins.then_inc(norm.sum, 1)

            pe.wait_ge(s_wgl, 1)
            out = ps[0:16, 0:2, :].rearrange("p b n -> p (b n)")
            for k in range(KT):
                pe.wait_ge(norms[0].lo, k + 1)
                ins = cross(out, act_hi[:, k, :], act_lo[:, k, :], wgl_hi[:, k, :], wgl_lo[:, k, :], k, k == 0, k == KT - 1)
            ins.then_inc(B.gl, 1)
            pe.wait_ge(s_setup, 1)
            sum_squares(norms[0], slot2(1))

            with pe.Fori(0, NBP) as i:
                def need(r):
                    if r == 0:
                        pe.wait_ge(B.free, i * 15 + 1)
                    elif 4 <= r < 14:
                        pe.wait_ge(B.free, i * 15 + (r - 2))
                    elif 14 <= r < 18:
                        pe.wait_ge(B.state, i * 31 + min(8 * (r - 13) + 1, 31))
                    elif r >= 18:
                        pe.wait_ge(B.free, i * 15 + (r - 6))

                def proj(r, t):
                    need(r)
                    project(slot2(r), t % 2, i * 6 + (N_B + t + 1))

                pe.wait_ge(norms[0].var, 1)
                proj(0, 0)
                proj(1, 1)
                need(2)
                pe.wait_ge(B.free, 1)
                pe.wait_ge(s_tab, 16 * 4)
                for st in range(ST):
                    ins = pe.matmul(slot2(2)[:, st * P:(st + 1) * P], glT[0:17, st * P:(st + 1) * P],
                                    wgu_sb[0:17, bass.ts(i, P)], start=True, stop=True)
                ins.then_inc(B.ready, 1)
                proj(3, 2)
                need(4)
                pe.wait_ge(B.la, i + 1)
                for st in range(ST):
                    ins = pe.matmul(slot2(4)[:, st * P:(st + 1) * P], b_la[:, st, :], cst[:, C_U:C_U + P],
                                    start=True, stop=True)
                ins.then_inc(B.ready, 1)
                proj(5, 3)
                need(6)
                pe.wait_ge(B.dec, i * 6 + 2)
                for st in range(ST):
                    ins = pe.transpose(slot2(6)[:, st * P:(st + 1) * P], b_kd[:, st * P:(st + 1) * P], ident)
                ins.then_inc(B.ready, 1)
                for h in range(2):
                    need(7 + h)
                    pe.wait_ge(B.free, i * 15 + (1 + (4 if h == 0 else 6)))
                    for st in range(ST):
                        ins = pe.transpose(slot2(7 + h)[:, st * P:(st + 1) * P], b_vt[:, h, st * P:(st + 1) * P], ident)
                    ins.then_inc(B.ready, 1)
                proj(9, 4)
                pe.wait_ge(B.free, i * 15 + 10)
                for g in range(4):
                    need(10 + g)
                    for c in range(4):
                        n = 4 * g + c
                        rows = slice(CH * (n % 2), CH * (n % 2) + CH)
                        col = kv_col(c)
                        ins = pe.matmul(slot2(10 + g)[:, col:col + 256], b_kdn[rows, n // 2, :],
                                        b_vn[rows, n // 2, :], start=True, stop=True)
                    ins.then_inc(B.ready, 1)
                proj(14, 5)
                pe.wait_ge(B.dec, i * 6 + 6)
                for h in range(2):
                    need(15 + h)
                    rows = slice(64 * h, 64 * h + 64)
                    for st in range(ST):
                        cols = slice(st * P, (st + 1) * P)
                        ins = pe.matmul(slot2(15 + h)[:, cols], b_k[rows, cols], b_q[rows, cols], start=True, stop=True)
                    ins.then_inc(B.ready, 1)
                pe.wait_ge(B.state, i * 31 + 31)
                for h in range(2):
                    need(17 + h)
                    pe.wait_ge(B.free, i * 15 + (13 + h))
                    rows = slice(64 * h, 64 * h + 64)
                    out = slot2(17 + h)
                    att = b_att if h == 0 else b_cum
                    for st in range(ST):
                        pe.matmul(out[:, st * P:(st + 1) * P], b_vn[:, st, h * P:(h + 1) * P], att[:, st * P:(st + 1) * P],
                                  start=True, stop=True, skip_group_check=True)
                        for n in (2 * st, 2 * st + 1):
                            ins = pe.matmul(out[:, n * CH:(n + 1) * CH], b_st[rows, n, :], b_qe[rows, n * CH:(n + 1) * CH],
                                            start=False, stop=True, skip_group_check=True)
                    ins.then_inc(B.ready, 1)
                for h in range(2):
                    need(19 + h)
                    pe.wait_ge(B.osq, i * 6 + 3 * h + 1)
                    for c in range(2):
                        ins = pe.matmul(slot2(19 + h)[:, c * HALF:(c + 1) * HALF], ones[:], b_v[:, c * HALF:(c + 1) * HALF],
                                        start=True, stop=True)
                    ins.then_inc(B.ready, 1)
                pe.wait_ge(B.o, i * 14 + 9)

            pe.wait_ge(B.free, 15 * NBP + 1)
            with pe.Fori(0, NHP // 2) as i:
                for e in range(2):
                    def at(per, c):
                        return i * (2 * per) + (per * e + c)

                    def proj(t, bank):
                        out = ps[:, bank:bank + 2, :].rearrange("p b n -> p (b n)")
                        project(out, (N_A + 3 * e + t) % 2, i * 6 + (N_A + 3 * e + t + 1))

                    proj(0, 0)
                    proj(1, 2)
                    pe.wait_ge(A.free, at(1, 1))
                    for st in range(ST):
                        ins = pe.transpose(slot2(2)[:, st * P:(st + 1) * P], a_vt[:, st * P:(st + 1) * P], ident)
                    ins.then_inc(A.ready, 1)
                    proj(2, 0)

                    def scores(u):
                        h, qt = u // 8, u % 8
                        rows = slice(64 * h, 64 * h + 64)
                        if u == 0:
                            pe.wait_ge(A.k, at(1, 1))
                            pe.wait_ge(A.q, at(1, 1))
                        if u == 1:
                            pe.wait_ge(A.vn, at(1, 1))
                        if u >= 2:
                            pe.wait_ge(A.max, at(16, u - 1))
                        out = slot2(1 + u % 2)
                        keys = (qt + 1) * P
                        for c in range(0, keys, HALF):
                            n = min(HALF, keys - c)
                            ins = pe.matmul(out[:, c:c + n], a_q[rows, qt * P:(qt + 1) * P], a_k[rows, c:c + n],
                                            start=True, stop=True)
                        ins.then_inc(A.s, 1)

                    scores(0)
                    scores(1)
                    for u in range(16):
                        h, qt = u // 8, u % 8
                        pe.wait_ge(A.p, at(16, u + 1))
                        for gi, g0 in enumerate(range(0, qt + 1, 4)):
                            g = groups_before(u) + gi
                            if g >= 2:
                                pe.wait_ge(A.ptf, at(24, g - 1))
                            for kt in range(g0, min(g0 + 4, qt + 1)):
                                ins = pe.transpose(ps[:, g % 2, (kt - g0) * P:(kt - g0 + 1) * P],
                                                   a_s[:, u % 2, kt * P:(kt + 1) * P], ident)
                            ins.then_inc(A.pt, 1)
                        if u + 2 < 16:
                            scores(u + 2)
                        pe.wait_ge(A.ptf, at(24, groups_before(u + 1)))
                        ob = u // 4
                        if u % 4 == 0 and ob >= 2:
                            pe.wait_ge(A.of, at(4, ob - 1))
                        for kt in range(qt + 1):
                            ins = pe.matmul(ps[64 * h:64 * h + 64, 6 + ob % 2, (qt % 4) * P:(qt % 4 + 1) * P],
                                            a_vn[:, kt, 64 * h:64 * h + 64], a_pt[:, u % 2, kt * P:(kt + 1) * P],
                                            start=(kt == 0), stop=(kt == qt))
                        ins.then_inc(A.pv, 1)

            def residual(O, base, before):
                before()
                for m in range(KT):
                    if m >= 4:
                        pe.wait_ge(O.added, m - 3)
                    project(slot2(m), (base + m) % 2, base + m + 1, O.lo if m == 0 else None)

            def before_wo():
                pe.wait_ge(A.of, 4 * NHP)
                pe.wait_ge(A.max, 16 * NHP)
                pe.wait_ge(A.ptf, 24 * NHP)

            residual(WO, N_WO, before_wo)

            def ffn(F, base, norm, prev):
                pe.wait_ge(prev.added, KT)

                def up(r, t, slot, split_done, lo_sem=None):
                    project(slot2(r), slot, split_done, lo_sem)

                def down(r0, par, ready_g, split_done, waits):
                    pe.wait_ge(F.glo, ready_g)
                    pe.wait_ge(s_wsplit, split_done)
                    for m in range(KT):
                        waits(r0 + m)
                        out = slot2(r0 + m)
                        for t in range(2):
                            ins = cross(out, g_hi[:, 2 * par + t, :], g_lo[:, 2 * par + t, :],
                                        w_hi[:, 2 + t, m * P:(m + 1) * P], w_lo[:, 2 + t, m * P:(m + 1) * P],
                                        m, t == 0, t == 1)
                        ins.then_inc(s_proj, 1)

                up(0, 0, 0, base + 1, norm.lo)
                sum_squares(norm, slot2(1))
                for t in range(1, 4):
                    if t == 3:
                        pe.wait_ge(F.free, 1)
                    up(t + 1, t, t, base + t + 1)
                with pe.Fori(0, (NBLK - 1) // 2) as i:
                    pe.wait_ge(norm.var, 1)
                    for par in range(2):
                        for t in range(4):
                            n = 4 + 12 * par + t
                            pe.wait_ge(F.free, i * 24 + (n - 3))
                            up(n + 1, t, t % 2, i * 12 + (base + 4 + 6 * par + t + 1))
                        down(4 + 12 * par + 4 + 1, par, i * 4 + (2 * par + 2), i * 12 + (base + 4 + 6 * par + 6),
                             lambda r: pe.wait_ge(F.free, i * 24 + (r - 4)))
                last = 4 + 12 * (NBLK - 1)
                down(last + 1, 0, FT, base + FFN_TILES, lambda r: pe.wait_ge(F.free, r - 4))

            ffn(f0, N_F0, norms[1], WO)
            F_TOTAL = 4 + 12 * (NBLK - 1) + 8
            pe.wait_ge(f0.free, F_TOTAL)

            def v_tile(half, st):
                n = 8 * half + st
                bank = n % 6
                if n >= 6:
                    pe.wait_ge(C.vf, n - 5)
                out = ps[:, bank, :]
                for k in range(KT):
                    slot, kk = k // 2, k % 2
                    if st == 0:
                        pe.wait_ge(s_wsplit, N_V + 4 * half + slot + 1)
                    if n == 0:
                        pe.wait_ge(norms[2].lo, k + 1)
                    cols = slice(kk * HALF, (kk + 1) * HALF)
                    pcols = slice(st * P, (st + 1) * P)
                    pe.matmul(out, act_hi[:, k, pcols], w_hi[:, slot, cols], start=(k == 0), stop=False)
                    pe.matmul(out, act_hi[:, k, pcols], w_lo[:, slot, cols], start=False, stop=False)
                    ins = pe.matmul(out, act_lo[:, k, pcols], w_hi[:, slot, cols], start=False, stop=(k == KT - 1))
                    if k == KT - 1:
                        ins.then_inc(s_proj, 1)
                    elif st == ST - 1 and kk == 1:
                        ins.then_inc(C.slot, 1)

            v_tile(0, 0)
            sum_squares(norms[2], slot2(3))
            v_tile(0, 1)
            v_tile(0, 2)
            v_tile(0, 3)
            pe.wait_ge(norms[2].rstd, 1)
            for st in range(ST):
                ins = pe.matmul(ps[:, 7, st:st + 1], rstd[0:1, st * P:(st + 1) * P], ones[0:1, 0:1], start=True, stop=True)
            ins.then_inc(C.rn, 1)
            for n in range(4, 16):
                v_tile(n // 8, n % 8)

            def c_u(r, m):
                if r >= 4:
                    pe.wait_ge(C.free, r - 3)
                project(slot2(r), (N_CU + m) % 2, N_CU + m + 1)

            pe.wait_ge(C.vf, 16)
            c_u(0, 0)
            c_u(1, 1)
            pe.wait_ge(C.rnf, 1)
            pe.wait_ge(C.ws, 1)
            pe.wait_ge(C.vn, ST)
            for g in range(KT):
                r = 2 + g
                if r >= 4:
                    pe.wait_ge(C.free, r - 3)
                for n in range(ST):
                    ins = pe.matmul(slot2(r)[:, n * P:(n + 1) * P], vs[:, g, n, :], wst[:, g, :], start=True, stop=True)
                ins.then_inc(C.ready, 1)
            for m in range(2, KT):
                c_u(8 + m, m)

            residual(WOC, N_WOC, lambda: pe.wait_ge(C.free, 16))
            ffn(f1, N_F1, norms[3], WOC)
            pe.wait_ge(f1.free, F_TOTAL)
            sum_squares(norms[4], slot2(0))

        @block.vector
        def _(dve):
            def carry_wait(j):
                dve.memset(carry[:, j:j + 1], 0.0)

            def norm_rstd(norm, psum):
                dve.wait_ge(norm.sum, 1)
                v, t = sq[:, 0, :], sq[:, 1, :]
                dve.tensor_scalar(v, psum, 1.0 / D, EPS, ALU.mult, ALU.add).then_inc(norm.var, 1)
                dve.wait_ge(norm.exp, 1)
                dve.scalar_tensor_tensor(t, v, -0.5, rstd[:], ALU.mult, ALU.mult).then_inc(norm.var, 1)
                dve.wait_ge(norm.var, 2)
                dve.tensor_tensor(v, t, rstd[:], ALU.mult).then_inc(norm.var, 1)
                dve.wait_ge(norm.var, 3)
                dve.scalar_tensor_tensor(rstd[:], v, 1.5, rstd[:], ALU.add, ALU.mult).then_inc(norm.rstd, 1)

            def accumulate(norm, k):
                dve.wait_ge(norm.sq, k + 1)
                if k:
                    dve.wait_ge(norm.acc, k)
                if k == 0:
                    dve.tensor_copy(acc[:], sq[:, 0, :]).then_inc(norm.acc, 1)
                else:
                    dve.tensor_tensor(acc[:], acc[:], sq[:, k % 2, :], ALU.add).then_inc(norm.acc, 1)

            def act_low(norm, k):
                dve.wait_ge(norm.hi, k + 1)
                dve.scalar_tensor_tensor(act_lo[:, k, :], x[:, k, :], gain[:, norm.col + k:norm.col + k + 1],
                                         act_hi[:, k, :].bitcast(F32), ALU.mult, ALU.subtract).then_inc(norm.lo, 1)

            dve.memset(ones[:], 1.0).then_inc(s_setup, 1)
            dve.memset(glT[0:32, :], 1.0).then_inc(s_rope_v, 1)
            for k in range(KT):
                act_low(norms[0], k)
                accumulate(norms[0], k)
            norm_rstd(norms[0], slot2(1))

            dve.wait_ge(B.gl, 1)
            dve.wait_ge(norms[0].rstd, 1)
            dve.wait_ge(s_rope_v, 1)
            dve.tensor_tensor(glT[0:16, :], ps[0:16, 0:2, :].rearrange("p b n -> p (b n)"), rstd[0:16, :],
                              ALU.mult).then_inc(B.free, 1)

            n_v = [1]

            def step(ins):
                ins.then_inc(s_rope_v, 1)
                n_v[0] += 1
                dve.wait_ge(s_rope_v, n_v[0])

            dve.wait_ge(s_tab, 16 * 4)
            step(dve.tensor_copy(r_a[:], pos_i[:]))
            step(dve.tensor_scalar(r_a[:], r_a[:], cst[:, C_INV:C_INV + 1], None, ALU.mult))
            step(dve.tensor_scalar(r_n[:], r_a[:], 1.0 / TWO_PI, MAGIC, ALU.mult, ALU.add))
            step(dve.tensor_scalar(r_n[:], r_n[:], -MAGIC, None, ALU.add))
            for part in PI_PARTS:
                step(dve.scalar_tensor_tensor(r_a[:], r_n[:], -part, r_a[:], ALU.mult, ALU.add))
            step(dve.tensor_scalar(r_a[:], r_a[:], 3.1415925, -3.1415925, ALU.min, ALU.max))
            dve.wait_ge(s_rope_a, 2)
            step(dve.scalar_tensor_tensor(ropeC[:], r_r[:], -2.0, r_r[:], ALU.mult, ALU.mult))
            dve.scalar_tensor_tensor(ropeC[:], ropeC[:], 1.0, rstd[:], ALU.add, ALU.mult).then_inc(s_rope_v, 1)
            dve.scalar_tensor_tensor(ropeS[:], ropeS[:], cst[:, C_SGN:C_SGN + 1], rstd[:], ALU.mult,
                                     ALU.mult).then_inc(s_rope_v, 1)
            n_v[0] += 2
            rope_done = n_v[0]

            with dve.Fori(0, NBP) as i:
                weights = (0, 1, 3, 5, 9, 14)

                def ready(r):
                    if r in weights:
                        dve.wait_ge(s_proj, i * 6 + (weights.index(r) + 1))
                    else:
                        dve.wait_ge(B.ready, i * 15 + (r + 1 - sum(w < r for w in weights)))

                def chunks(t):
                    return t.rearrange("p (n c) -> p n c", c=CH)

                def at(t, c):
                    return chunks(t)[:, :, c:c + 1].to_broadcast([P, NCH, CH])

                ready(0)
                dve.tensor_tensor(b_k[:], slot2(0), rstd[:], ALU.mult).then_inc(B.free, 1)
                ready(1)
                dve.tensor_tensor(b_q[:], slot2(1), rstd[:], ALU.mult).then_inc(B.free, 1)
                ready(2)
                dve.tensor_scalar(b_cum[:], slot2(2), 0.0, None, ALU.min).then_inc(B.min, 1)
                dve.wait_ge(B.min, i + 1)
                dve.scalar_tensor_tensor(b_e[:], b_cum[:], 2.0, slot2(2), ALU.mult, ALU.subtract).then_inc(B.free, 1)
                dve.wait_ge(B.e, i * 6 + 2)
                dve.wait_ge(B.free, i * 15 + 4)
                dve.tensor_tensor(b_la[:].rearrange("p a b -> p (a b)"), b_cum[:], b_e[:], ALU.subtract).then_inc(B.la, 1)
                ready(3)
                dve.tensor_tensor(b_vt[:, 0, :], slot2(3), rstd[:], ALU.mult).then_inc(B.free, 1)
                ready(4)
                dve.tensor_copy(b_cum[:], slot2(4)).then_inc(B.free, 1)
                dve.wait_ge(B.free, i * 15 + 6)
                dve.tensor_tensor(chunks(b_e[:]), at(b_cum[:], CH - 1), chunks(b_cum[:]), ALU.subtract).then_inc(B.dec, 1)
                dve.wait_ge(B.e, i * 6 + 3)
                dve.tensor_tensor(b_kd[:], b_k[:], b_e[:], ALU.mult).then_inc(B.dec, 1)
                ready(5)
                dve.tensor_tensor(b_vt[:, 1, :], slot2(5), rstd[:], ALU.mult).then_inc(B.free, 1)
                dve.wait_ge(B.dec, i * 6 + 2)
                dve.tensor_tensor(chunks(b_e[:]), chunks(b_cum[:]), at(b_cum[:], CH // 2 - 1), ALU.subtract).then_inc(B.dec, 1)
                dve.wait_ge(B.e, i * 6 + 6)
                dve.scalar_tensor_tensor(b_qe[:], b_q[:], A_SCALE, b_cum[:], ALU.mult, ALU.mult).then_inc(B.dec, 1)
                dve.scalar_tensor_tensor(b_q[:], b_q[:], A_SCALE, b_v[:], ALU.mult, ALU.mult).then_inc(B.dec, 1)
                dve.tensor_tensor(b_k[:], b_k[:], b_e[:], ALU.mult).then_inc(B.dec, 1)
                ready(6)
                dve.tensor_copy(b_kdn[:].rearrange("p a b -> p (a b)"), slot2(6)).then_inc(B.free, 1)
                for h in range(2):
                    ready(7 + h)
                    dve.tensor_copy(b_vn[:, :, h * P:(h + 1) * P], slot2(7 + h).rearrange("p (a b) -> p a b", b=P)
                                    ).then_inc(B.free, 1)
                ready(9)
                dve.tensor_tensor(b_r[:, 0, :], slot2(9), rstd[:], ALU.mult).then_inc(B.free, 1)
                dve.memset(b_st[:, 0, :], 0.0).then_inc(B.state, 1)
                dve.memset(b_att[:], 0.0).then_inc(B.o, 1)
                for g in range(4):
                    ready(10 + g)
                    kv = slot2(10 + g)
                    for c in range(4):
                        n = 4 * g + c
                        if n == NCH - 1:
                            break
                        dve.wait_ge(B.state, i * 31 + (2 * n + 1))
                        for h in range(2):
                            rows = slice(64 * h, 64 * h + 64)
                            ins = dve.scalar_tensor_tensor(
                                b_st[rows, n + 1, :], b_st[rows, n, :], b_cum[rows, n * CH + CH - 1:(n + 1) * CH],
                                kv[rows, kv_col(c) + h * P:kv_col(c) + (h + 1) * P], ALU.mult, ALU.add)
                            ins.then_inc(B.state, 1)
                ready(14)
                dve.tensor_tensor(b_r[:, 1, :], slot2(14), rstd[:], ALU.mult).then_inc(B.free, 1)
                mask = cst[:, C_M64:C_M64 + P].bitcast(U32)
                dve.wait_ge(B.state, i * 31 + 31)
                dve.memset(b_cum[:], 0.0).then_inc(B.o, 1)
                dve.wait_ge(B.o, i * 14 + 2)
                for h in range(2):
                    ready(15 + h)
                    carry_wait(h)
                    att = b_att if h == 0 else b_cum
                    for c in range(ST):
                        ins = dve.copy_predicated(att[:, c * P:(c + 1) * P], mask, slot2(15 + h)[:, c * P:(c + 1) * P])
                    ins.then_inc(B.free, 1)
                for h in range(2):
                    ready(17 + h)
                    dve.tensor_copy(b_k[:] if h == 0 else b_q[:], slot2(17 + h)).then_inc(B.free, 1)
                for h in range(2):
                    o = b_k if h == 0 else b_q
                    v, y, t = b_e, b_kd, b_qe
                    c0 = i * 14 + (2 + 6 * h)
                    ready(19 + h)
                    dve.tensor_scalar(v[:], slot2(19 + h), 1.0 / P, EPS, ALU.mult, ALU.add).then_inc(B.o, 1)
                    dve.wait_ge(B.osq, i * 6 + (3 * h + 3))
                    dve.scalar_tensor_tensor(t[:], v[:], -0.5, y[:], ALU.mult, ALU.mult).then_inc(B.o, 1)
                    dve.wait_ge(B.o, c0 + 2)
                    dve.tensor_tensor(t[:], t[:], y[:], ALU.mult).then_inc(B.o, 1)
                    dve.wait_ge(B.o, c0 + 3)
                    dve.scalar_tensor_tensor(y[:], t[:], 1.5, y[:], ALU.add, ALU.mult).then_inc(B.o, 1)
                    dve.wait_ge(B.o, c0 + 4)
                    dve.scalar_tensor_tensor(t[:], o[:], gain[:, G_OUT:G_OUT + 1], y[:], ALU.mult, ALU.mult).then_inc(B.o, 1)
                    dve.wait_ge(B.o, c0 + 5)
                    dve.wait_ge(B.silu, i * 2 + (h + 1))
                    dve.tensor_tensor(oT[:, bass.ds(i * 2 + (4 + h), 1), :].rearrange("p a n -> p (a n)"), t[:],
                                      b_r[:, h, :], ALU.mult).then_inc(B.o, 1)

            dve.wait_ge(s_rope_v, rope_done)
            with dve.Fori(0, NHP // 2) as i:
                for e in range(2):
                    def at(per, c):
                        return i * (2 * per) + (per * e + c)

                    dve.wait_ge(s_proj, i * 6 + (R_A + 3 * e + 1))
                    dve.tensor_tensor(a_vt[:], slot2(0), rstd[:], ALU.mult).then_inc(A.free, 1)

                    def rope(psum, out, sh, n0, done):
                        carry_wait(0 if n0 == 0 else 1)
                        dve.stream_shuffle(sh[:], psum, [(j + 8) % 16 if j < 16 else j for j in range(32)]
                                           ).then_inc(A.rope, 1)
                        dve.tensor_tensor(out[:], psum, ropeC[:], ALU.mult).then_inc(A.rope, 1)
                        dve.wait_ge(A.rope, at(6, n0 + 1))
                        dve.tensor_tensor(sh[:], sh[:], ropeS[:], ALU.mult).then_inc(A.rope, 1)
                        dve.wait_ge(A.rope, at(6, n0 + 3))
                        dve.tensor_tensor(out[:], out[:], sh[:], ALU.add).then_inc(done, 1)

                    dve.wait_ge(s_proj, i * 6 + (R_A + 3 * e + 2))
                    rope(slot2(1), a_k, a_sh, 0, A.k)
                    dve.wait_ge(s_proj, i * 6 + (R_A + 3 * e + 3))
                    rope(slot2(0), a_q, a_t, 3, A.q)

                    def top(u):
                        keys = (u % 8 + 1) * P
                        dve.wait_ge(A.s, at(16, u + 1))
                        carry_wait(2 + u % 2)
                        dve.tensor_tensor_reduce(a_s[:, u % 2, 0:keys], slot2(1 + u % 2)[:, 0:keys],
                                                 lmul[:, S - keys:S], -A_SCALE, 1e30, ALU.add, ALU.min,
                                                 tiny[:, 8 + u % 2:9 + u % 2]).then_inc(A.max, 1)

                    def scale(u):
                        keys = (u % 8 + 1) * P
                        dve.wait_ge(A.e, at(16, u + 1))
                        dve.reciprocal(tiny[:, 16 + u % 2:17 + u % 2], tiny[:, 12 + u % 2:13 + u % 2]).then_inc(A.rl, 1)
                        dve.wait_ge(A.rl, at(16, u + 1))
                        dve.tensor_scalar(a_s[:, u % 2, 0:keys], a_s[:, u % 2, 0:keys],
                                          tiny[:, 16 + u % 2:17 + u % 2], None, ALU.mult).then_inc(A.p, 1)

                    top(0)
                    for u in range(16):
                        if u + 1 < 16:
                            top(u + 1)
                        scale(u)

            def residual(O, res, norm, reload):
                for k in range(KT):
                    dve.wait_ge(O.hi, k + 1)
                    src = oT if O is WO else vs
                    t = src[:, k, :] if O is WO else src[:, k, :, :].rearrange("p a b -> p (a b)")
                    dve.tensor_tensor(act_lo[:, k, :], t, act_hi[:, k, :].bitcast(F32), ALU.subtract).then_inc(O.lo, 1)
                if reload:
                    dve.wait_ge(s_xr, 16 * KT)
                for m in range(KT):
                    dve.wait_ge(s_proj, res + m + 1)
                    dve.tensor_tensor(x[:, m, :], x[:, m, :], slot2(m), ALU.add).then_inc(O.added, 1)
                    if m:
                        accumulate(norm, m - 1)
                accumulate(norm, KT - 1)
                for k in range(KT):
                    act_low(norm, k)

            residual(WO, R_WO, norms[1], True)

            def ffn(F, layer, res, norm, nxt, last):
                def up(n, r_slot, g):
                    dve.wait_ge(s_proj, n)
                    dve.tensor_tensor(fz[:, g, :], slot2(r_slot), rstd[:], ALU.mult).then_inc(F.free, 1)

                def taps(g, cid, tap0, tile):
                    dve.wait_ge(F.cid, cid)
                    c1 = cw[:, layer, bass.ds(tile, 1), 1:2].rearrange("p a b -> p (a b)")
                    c0 = cw[:, layer, bass.ds(tile, 1), 0:1].rearrange("p a b -> p (a b)")
                    dve.scalar_tensor_tensor(fc[:, g, 1:S], fz[:, g, 0:S - 1], c1, fc[:, g, 1:S],
                                             ALU.mult, ALU.add).then_inc(F.tap, 1)
                    dve.wait_ge(F.tap, tap0 + 1)
                    dve.scalar_tensor_tensor(fc[:, g, 2:S], fz[:, g, 0:S - 2], c0, fc[:, g, 2:S],
                                             ALU.mult, ALU.add).then_inc(F.tap, 1)

                def gate(tap, j, par, t):
                    dve.wait_ge(F.tap, tap)
                    dve.wait_ge(F.silu, j)
                    dve.tensor_tensor(fc[:, 1, :], fz[:, 0, :], fc[:, 1, :], ALU.mult).then_inc(F.gated, 1)
                    dve.wait_ge(F.ghi, j)
                    dve.tensor_tensor(g_lo[:, 2 * par + t, :], fc[:, 1, :], g_hi[:, 2 * par + t, :].bitcast(F32),
                                      ALU.subtract).then_inc(F.glo, 1)

                norm_rstd(norm, slot2(1))
                dve.wait_ge(norm.rstd, 1)
                for t in range(4):
                    up(res + t + 1, 0 if t == 0 else t + 1, t % 2)
                    taps(t % 2, t + 1, 2 * t, t)
                    if t % 2:
                        gate(2 * t + 2, t // 2 + 1, 0, t // 2)
                with dve.Fori(0, (NBLK - 1) // 2) as i:
                    for par in range(2):
                        for t in range(4):
                            n = 4 + 12 * par + t
                            u = 4 + 4 * par + t
                            up(i * 24 + (res + n + 1), n + 1, t % 2)
                            taps(t % 2, i * 8 + (u + 1), i * 16 + 2 * u, i * 8 + u)
                            if t % 2:
                                gate(i * 16 + (2 * u + 2), i * 4 + (u // 2 + 1), 1 - par, t // 2)
                        for m in range(KT):
                            n = 4 + 12 * par + 4 + m
                            dve.wait_ge(s_proj, i * 24 + (res + n + 1))
                            dve.tensor_tensor(x[:, m, :], x[:, m, :], slot2(n + 1), ALU.add).then_inc(F.free, 1)
                base = 4 + 12 * (NBLK - 1)
                for m in range(KT):
                    dve.wait_ge(s_proj, res + base + m + 1)
                    dve.tensor_tensor(x[:, m, :], x[:, m, :], slot2(base + m + 1), ALU.add).then_inc(F.free, 1)
                    if m:
                        if not last:
                            act_low(nxt, m - 1)
                        accumulate(nxt, m - 1)
                if not last:
                    act_low(nxt, KT - 1)
                accumulate(nxt, KT - 1)

            ffn(f0, 0, R_F0, norms[1], norms[2], False)

            norm_rstd(norms[2], slot2(3))
            dve.wait_ge(C.rn, 1)
            dve.tensor_copy(tiny[:, 20:28], ps[:, 7, 0:8]).then_inc(C.rnf, 1)
            dve.wait_ge(s_cmx, 16 * 2)
            dve.tensor_tensor(wst[:], wst[:], cst[:, None, C_TRIL:C_TRIL + P].to_broadcast([P, KT, P]), ALU.mult).then_inc(C.ws, 1)
            dve.wait_ge(C.vsq, 16)
            sums = tiny[:, 28:44]
            v8, y8, t8 = tiny[:, 44:52], tiny[:, 52:60], tiny[:, 0:8]
            dve.tensor_tensor(v8, sums[:, 0:8], sums[:, 8:16], ALU.add).then_inc(C.t, 1)
            dve.wait_ge(C.t, 1)
            dve.tensor_scalar(v8, v8, 1.0 / D, EPS, ALU.mult, ALU.add).then_inc(C.t, 1)
            dve.wait_ge(C.ta, 2)
            dve.scalar_tensor_tensor(t8, v8, -0.5, y8, ALU.mult, ALU.mult).then_inc(C.t, 1)
            dve.wait_ge(C.t, 3)
            dve.tensor_tensor(t8, t8, y8, ALU.mult).then_inc(C.t, 1)
            dve.wait_ge(C.t, 4)
            dve.scalar_tensor_tensor(y8, t8, 1.5, y8, ALU.add, ALU.mult).then_inc(C.t, 1)
            dve.wait_ge(C.t, 5)
            for st in range(ST):
                dve.tensor_scalar(vs[:, :, st, :], vs[:, :, st, :], y8[:, st:st + 1], None, ALU.mult).then_inc(C.vn, 1)

            def c_scale(r, m):
                dve.wait_ge(s_proj, R_CU + m + 1)
                if m >= 2:
                    dve.wait_ge(C.gated, m - 1)
                dve.tensor_tensor(cz[:, m % 2, :], slot2(r), rstd[:], ALU.mult).then_inc(C.free, 1)

            def c_gate(m):
                dve.wait_ge(C.u, m + 1)
                t = vs[:, m, :, :].rearrange("p a b -> p (a b)")
                dve.tensor_tensor(t, t, cz[:, m % 2, :], ALU.mult).then_inc(C.gated, 1)

            c_scale(0, 0)
            c_scale(1, 1)
            for g in range(KT):
                r = 2 + g
                dve.wait_ge(C.ready, g + 1)
                dve.scalar_tensor_tensor(vs[:, g, :, :], slot2(r).rearrange("p (a b) -> p a b", b=P),
                                         gain[:, G_SGU + g:G_SGU + g + 1],
                                         bspb[:, None, g * P:(g + 1) * P].to_broadcast([P, ST, P]),
                                         ALU.mult, ALU.add).then_inc(C.free, 1)
            dve.wait_ge(C.free, 10)
            c_gate(0)
            c_gate(1)
            for m in range(2, KT):
                c_scale(8 + m, m)
                c_gate(m)

            residual(WOC, R_WOC, norms[3], False)
            ffn(f1, 1, R_F1, norms[3], norms[4], True)
            norm_rstd(norms[4], slot2(0))
            dve.wait_ge(norms[4].rstd, 1)
            for k in range(KT):
                dve.scalar_tensor_tensor(x[:, k, :], x[:, k, :], gain[:, G_FIN + k:G_FIN + k + 1], rstd[:], ALU.mult,
                                         ALU.mult).then_inc(s_fin, 1)

        @block.scalar
        def _(act):
            def guess(norm):
                act.wait_ge(norm.var, 1)
                act.activation(rstd[:], sq[:, 0, :], ACT.Ln).then_inc(norm.ln, 1)
                act.wait_ge(norm.ln, 1)
                act.activation(rstd[:], rstd[:], ACT.Exp, scale=-0.5).then_inc(norm.exp, 1)

            def high(norm, k):
                act.activation(act_hi[:, k, :], x[:, k, :], ACT.Copy, scale=gain[:, norm.col + k:norm.col + k + 1]
                               ).then_inc(norm.hi, 1)

            def square(norm, k):
                if k >= 2:
                    act.wait_ge(norm.acc, k - 1)
                act.activation(sq[:, k % 2, :], x[:, k, :], ACT.Square).then_inc(norm.sq, 1)

            act.wait_ge(s_cst, 16 * 3)
            for k in range(KT):
                act.wait_ge(s_x[k], 16)
                high(norms[0], k)
                square(norms[0], k)
            guess(norms[0])

            act.wait_ge(s_rope_v, 10)
            act.activation(ropeS[:], r_a[:], ACT.Sin).then_inc(s_rope_a, 1)
            act.activation(r_r[:], r_a[:], ACT.Sin, scale=0.5).then_inc(s_rope_a, 1)

            with act.Fori(0, NBP) as i:
                act.wait_ge(B.free, i * 15 + 4)
                act.activation(b_e[:], b_e[:], ACT.Exp).then_inc(B.e, 1)
                act.wait_ge(B.e, i * 6 + 1)
                act.activation(b_e[:], b_e[:], ACT.Ln, bias=1.0).then_inc(B.e, 1)
                act.wait_ge(B.dec, i * 6 + 1)
                act.activation(b_e[:], b_e[:], ACT.Exp).then_inc(B.e, 1)
                act.wait_ge(B.dec, i * 6 + 3)
                act.activation(b_v[:], b_e[:], ACT.Exp).then_inc(B.e, 1)
                act.wait_ge(B.e, i * 6 + 4)
                act.activation(b_e[:], b_e[:], ACT.Exp, scale=-1.0).then_inc(B.e, 1)
                act.activation(b_cum[:], b_cum[:], ACT.Exp).then_inc(B.e, 1)
                for h in range(2):
                    act.wait_ge(B.free, i * 15 + (11 + h))
                    act.activation(b_r[:, h, :], b_r[:, h, :], ACT.Silu).then_inc(B.silu, 1)
                for h in range(2):
                    act.wait_ge(B.free, i * 15 + (15 + h))
                    if h == 1:
                        act.wait_ge(B.ready, i * 15 + 14)
                    act.activation(b_v[:], (b_k if h == 0 else b_q)[:], ACT.Square).then_inc(B.osq, 1)
                    act.wait_ge(B.o, i * 14 + (2 + 6 * h + 1))
                    act.activation(b_kd[:], b_e[:], ACT.Ln).then_inc(B.osq, 1)
                    act.wait_ge(B.osq, i * 6 + (3 * h + 2))
                    act.activation(b_kd[:], b_kd[:], ACT.Exp, scale=-0.5).then_inc(B.osq, 1)

            with act.Fori(0, NHP // 2) as i:
                for e in range(2):
                    def at(per, c):
                        return i * (2 * per) + (per * e + c)

                    act.wait_ge(A.ready, at(1, 1))
                    act.activation(a_vn[:].rearrange("p a b -> p (a b)"), slot2(2), ACT.Copy).then_inc(A.vn, 1)

                    def exp(u):
                        keys = (u % 8 + 1) * P
                        act.wait_ge(A.max, at(16, u + 1))
                        act.activation(a_s[:, u % 2, 0:keys], a_s[:, u % 2, 0:keys], ACT.Exp, scale=-1.0,
                                       bias=tiny[:, 8 + u % 2:9 + u % 2], accum_out=tiny[:, 12 + u % 2:13 + u % 2]
                                       ).then_inc(A.e, 1)

                    def take(u):
                        qt = u % 8
                        for gi, g0 in enumerate(range(0, qt + 1, 4)):
                            g = groups_before(u) + gi
                            n = min(g0 + 4, qt + 1) - g0
                            act.wait_ge(A.pt, at(24, g + 1))
                            if u >= 2:
                                act.wait_ge(A.pv, at(16, u - 1))
                            act.activation(a_pt[:, u % 2, g0 * P:(g0 + n) * P], ps[:, g % 2, 0:n * P], ACT.Copy
                                           ).then_inc(A.ptf, 1)

                    def out(u):
                        h, ob = u // 8, u // 4
                        act.wait_ge(A.pv, at(16, u + 1))
                        rows = slice(64 * h, 64 * h + 64)
                        act.activation(oT[rows, bass.ds(i * 2 + e, 1), (ob % 2) * HALF:(ob % 2 + 1) * HALF
                                          ].rearrange("p a n -> p (a n)"), ps[rows, 6 + ob % 2, :], ACT.Copy
                                       ).then_inc(A.of, 1)

                    exp(0)
                    for u in range(16):
                        if u + 1 < 16:
                            exp(u + 1)
                        take(u)
                        if u % 4 == 0 and u:
                            out(u - 1)
                    out(15)

            act.wait_ge(A.of, 4 * NHP)
            for k in range(KT):
                act.dma_start(x[:, k, :], xT[k]).then_inc(s_xr, 16)

            def residual(O, norm, src):
                for k in range(KT):
                    if O is WOC:
                        act.wait_ge(C.gated, k + 1)
                        if k == 0:
                            act.wait_ge(s_proj, R_WOC)
                    act.activation(act_hi[:, k, :], src(k), ACT.Copy).then_inc(O.hi, 1)
                for m in range(KT):
                    act.wait_ge(O.added, m + 1)
                    square(norm, m)
                for k in range(KT):
                    high(norm, k)

            act.wait_ge(B.o, 14 * NBP)
            residual(WO, norms[1], lambda k: oT[:, k, :])

            def ffn(F, layer, norm, nxt, last):
                def start(g, n, tile_w, tile_b, cu_free):
                    act.wait_ge(F.free, n)
                    if cu_free is not None:
                        act.wait_ge(F.glo, cu_free)
                    act.activation(fc[:, g, :], fz[:, g, :], ACT.Identity, scale=tile_w, bias=tile_b).then_inc(F.cid, 1)

                def silu(tap):
                    act.wait_ge(F.tap, tap)
                    act.activation(fz[:, 0, :], fc[:, 0, :], ACT.Silu).then_inc(F.silu, 1)

                def g_high(j, par, t):
                    act.wait_ge(F.gated, j)
                    act.activation(g_hi[:, 2 * par + t, :], fc[:, 1, :], ACT.Copy).then_inc(F.ghi, 1)

                guess(norm)
                for t in range(4):
                    start(t % 2, t + 1, cw[:, layer, t, 2:3], cw[:, layer, t, 3:4], 1 if t == 3 else None)
                    if t % 2 == 0:
                        silu(2 * t + 2)
                    else:
                        g_high(t // 2 + 1, 0, t // 2)
                with act.Fori(0, (NBLK - 1) // 2) as i:
                    for par in range(2):
                        for t in range(4):
                            n = 4 + 12 * par + t
                            u = 4 + 4 * par + t
                            tile = i * 8 + u
                            start(t % 2, i * 24 + (n + 1),
                                  cw[:, layer, bass.ds(tile, 1), 2:3].rearrange("p a b -> p (a b)"),
                                  cw[:, layer, bass.ds(tile, 1), 3:4].rearrange("p a b -> p (a b)"),
                                  i * 4 + u // 2 if t % 2 else None)
                            if t % 2 == 0:
                                silu(i * 16 + (2 * u + 2))
                            else:
                                g_high(i * 4 + (u // 2 + 1), 1 - par, t // 2)
                base = 4 + 12 * (NBLK - 1)
                for m in range(KT):
                    act.wait_ge(F.free, base + m + 1)
                    if not last:
                        high(nxt, m)
                    square(nxt, m)

            ffn(f0, 0, norms[1], norms[2], False)

            guess(norms[2])
            act.wait_ge(C.rnf, 1)
            for n in range(16):
                half, st = n // 8, n % 8
                act.wait_ge(s_proj, R_V + n + 1)
                vv = vs[:, 4 * half:4 * half + 4, st, :]
                act.activation(vv, ps[:, n % 6, :].rearrange("p (a b) -> p a b", b=P), ACT.Gelu_apprx_tanh,
                               scale=tiny[:, 20 + st:21 + st]).then_inc(C.vf, 1)
                act.wait_ge(C.vf, n + 1)
                act.activation(sq[:, 0, 0:HALF].rearrange("p (a b) -> p a b", b=P), vv, ACT.Square,
                               accum_out=tiny[:, 28 + n:29 + n]).then_inc(C.vsq, 1)
            act.wait_ge(C.t, 2)
            act.activation(tiny[:, 52:60], tiny[:, 44:52], ACT.Ln).then_inc(C.ta, 1)
            act.wait_ge(C.ta, 1)
            act.activation(tiny[:, 52:60], tiny[:, 52:60], ACT.Exp, scale=-0.5).then_inc(C.ta, 1)
            for m in range(KT):
                act.wait_ge(C.free, m + 1 if m < 2 else 8 + m + 1)
                act.activation(cz[:, m % 2, :], cz[:, m % 2, :], ACT.Gelu_apprx_tanh).then_inc(C.u, 1)
            residual(WOC, norms[3], lambda k: vs[:, k, :, :].rearrange("p a b -> p (a b)"))
            ffn(f1, 1, norms[3], norms[4], True)
            guess(norms[4])


def kernel(x, positions, norm_mix, norm_ffn, w_in_ab, w_gate_up, b_gate_up, g_out_b, w_out_ab, w_in_c, g_sgu,
           w_spatial, b_spatial, w_out_c, w_up, conv_w, conv_b, w_down, norm_final):
    import concourse.bacc as bacc
    from concourse.bass_utils import run_bass_kernel_spmd

    def tiles(w):
        n = w.shape[1] // P
        return np.ascontiguousarray(w.reshape(KT, P, n, P).transpose(2, 1, 0, 3)).reshape(n, P, KT * P)

    def cols(v):
        return v.reshape(-1, P).T

    x, w_in_ab, w_in_c = np.asarray(x), np.asarray(w_in_ab)[0], np.asarray(w_in_c)[0]
    w_up, conv_w, conv_b = np.asarray(w_up), np.asarray(conv_w), np.asarray(conv_b)
    norm_mix, norm_ffn = np.asarray(norm_mix), np.asarray(norm_ffn)
    c, logmul = constant_arrays()
    gains = np.concatenate([cols(norm_mix[0]), cols(norm_mix[1]), cols(norm_ffn[0]), cols(norm_ffn[1]),
                            cols(np.asarray(norm_final)), cols(np.asarray(g_sgu)), cols(np.asarray(g_out_b))], axis=1)
    up = w_up.reshape(2, KT, P, 2, FT, P).transpose(0, 4, 3, 2, 1, 5).reshape(2, 2 * FT, P, KT * P)
    taps = np.concatenate([conv_w, conv_b[:, None]], axis=1)
    taps = taps.reshape(2, 4, 2, FT, P).transpose(4, 0, 3, 2, 1).reshape(P, 2, 2 * FT, 4)
    wv = w_in_c[:, D:].reshape(4, 2, P, 2, HALF).transpose(3, 0, 2, 1, 4).reshape(8, P, 2 * HALF)
    arrays = {
        "xT": x[0].T.reshape(KT, P, S),
        "pos": np.asarray(positions).reshape(1, S),
        "consts": c,
        "logmul": logmul,
        "gains": gains,
        "wgu": np.asarray(w_gate_up)[0],
        "bgu": np.asarray(b_gate_up).reshape(1, 256),
        "wgl": w_in_ab[:, 3072:].reshape(KT, P, 16).transpose(1, 0, 2).reshape(P, KT * 16),
        "w_in": tiles(w_in_ab[:, :3072]),
        "w_out": tiles(np.asarray(w_out_ab)[0]),
        "w_u": tiles(w_in_c[:, :D]),
        "w_v": wv,
        "w_outc": tiles(np.asarray(w_out_c)[0]),
        "wsT": np.asarray(w_spatial)[0].transpose(2, 0, 1),
        "bsp": np.asarray(b_spatial).reshape(1, KT * P),
        "w_up": up,
        "w_dn": np.asarray(w_down).reshape(2, FT, P, D),
        "conv": taps,
    }
    arrays = {n: np.ascontiguousarray(a) for n, a in arrays.items()}
    nc = bacc.Bacc("TRN2", target_bir_lowering=False, num_devices=1)
    args = [nc.dram_tensor(n, a.shape, mybir.dt.from_np(a.dtype), kind="ExternalInput").ap() for n, a in arrays.items()]
    args.append(nc.dram_tensor("outT", (KT, P, S), F32, kind="ExternalOutput").ap())
    build(nc, *args)
    r = run_bass_kernel_spmd(nc, [arrays], core_ids=[0])
    out = r.results[0]["outT"]
    return np.ascontiguousarray(out.reshape(D, S).T).reshape(1, S, D)
```

```python
from contextlib import ExitStack

import numpy as np

import concourse.bass as bass
from concourse import mybir

F32 = mybir.dt.float32
F32R = mybir.dt.float32r
I32 = mybir.dt.int32
U32 = mybir.dt.uint32
ALU = mybir.AluOpType
ACT = mybir.ActivationFunctionType

P = 128
D = 1024
S = 1024
HALF = 512
KT = D // P
ST = S // P
NHP = 4
NBP = 2
CH = 64
NCH = S // CH
FT = 2816 // P
NBLK = FT // 2
ROT = 16
THETA = 500000.0
EPS = 1e-6
A_SCALE = 0.125
TAU = 16.0
NEG = -1e30
BRANCHES = ((128, 1), (512, 4), (2048, 16))

QA, KA, VA, QB, KB, VB, RB = 0, 4, 8, 12, 14, 16, 20

C_ID, C_U, C_TRIL, C_M64, C_INV, C_SGN, C_N = 0, 128, 256, 384, 512, 513, 514
G_MIX0, G_MIX1, G_FFN0, G_FFN1, G_FIN, G_SGU, G_OUT, G_N = 0, 8, 16, 24, 32, 40, 48, 49

TWO_PI = 2.0 * np.pi
PI_PARTS = []
_rest = TWO_PI
for _k in range(3):
    _e = 2.0 ** (np.floor(np.log2(_rest)) - 7)
    _c = float(np.floor(_rest / _e) * _e)
    PI_PARTS.append(_c)
    _rest -= _c
PI_PARTS.append(float(np.float32(_rest)))
MAGIC = 12582912.0


def constant_arrays():
    c = np.zeros((P, C_N), np.float32)
    p = np.arange(P)
    c[:, C_ID:C_ID + P] = np.eye(P)
    same = (p[:, None] // CH) == (p[None, :] // CH)
    upper = p[:, None] <= p[None, :]
    c[:, C_U:C_U + P] = (same & upper) / TAU
    c[:, C_TRIL:C_TRIL + P] = upper
    c[:, C_M64:C_M64 + P] = same & upper
    half = ROT // 2
    r = p % 64
    inv = np.float32(THETA) ** (-np.arange(half, dtype=np.float32) * np.float32(2.0 / ROT))
    c[:, C_INV] = np.where(r < ROT, inv[r % half], 0.0)
    c[:, C_SGN] = np.where(r < half, -1.0, np.where(r < ROT, 1.0, 0.0))
    d = (ST - 1) * P + p[:, None] - np.arange(S)[None, :]
    count = np.zeros((P, S), np.float64)
    for window, dil in BRANCHES:
        count += (d >= 0) & (d <= window) & (d % dil == 0)
    m = np.where(count > 0, np.log(np.maximum(count, 1.0)) / A_SCALE, NEG)
    return c, m.astype(np.float32)


def build(nc, xT, pos, consts, logmul, gains, wgu, bgu, wgl, w_in, w_out, w_u, w_v, w_outc, wsT, bsp,
          w_up, w_dn, conv, outT):
    with ExitStack() as ctx:
        arena = -(-nc.sbuf_base // 64) * 64

        def sb(name, kb, shape, dt=F32):
            return nc.alloc_sbuf_tensor_at(name, shape, dt, offset=arena + int(kb * 1024))

        def sem(name):
            return ctx.enter_context(nc.semaphore(name))

        act_hi = sb("act_hi", 0, [P, KT, S], F32R)
        act_lo = sb("act_lo", 32, [P, KT, S], F32R)
        w_hi = sb("w_hi", 64, [P, 4, 1024], F32R)
        w_lo = sb("w_lo", 80, [P, 4, 1024], F32R)
        w_raw = sb("w_raw", 96, [P, 2, 1024])
        x = sb("x", 104, [P, KT, S])
        rstd = sb("rstd", 168, [P, S])
        sq = sb("sq", 172, [P, 2, S])
        acc = sb("acc", 180, [P, S])
        cst = sb("cst", 200, [P, C_N])
        gain = sb("gain", 202.25, [P, G_N])
        ones = sb("ones", 202.5, [P, P])
        cw = sb("cw", 203, [P, 2, 2 * FT, 4])
        tiny = sb("tiny", 204.5, [P, 64])
        carry = sb("carry", 204.75, [P, 4])
        g_hi = sb("g_hi", 136, [P, 4, S], F32R)
        g_lo = sb("g_lo", 152, [P, 4, S], F32R)
        fz = sb("fz", 184, [P, 2, S])
        fc = sb("fc", 192, [P, 2, S])
        oT = sb("oT", 136, [P, KT, S])
        vs = sb("vs", 136, [P, KT, ST, P])
        cz = sb("cz", 184, [P, 2, S])
        bspb = sb("bspb", 192, [P, KT * P])
        wst = sb("wst", 196, [P, KT, P])
        ropeC = sb("ropeC", 184, [P, S])
        ropeS = sb("ropeS", 188, [P, S])
        lmul = sb("lmul", 192, [P, S])
        glT = sb("glT", 196, [P, S])
        scr = [104 + 4 * i for i in range(8)]
        b_k, b_q = sb("b_k", scr[0], [P, S]), sb("b_q", scr[1], [P, S])
        b_cum, b_e = sb("b_cum", scr[2], [P, S]), sb("b_e", scr[3], [P, S])
        b_kd, b_qe = sb("b_kd", scr[4], [P, S]), sb("b_qe", scr[5], [P, S])
        b_vn = sb("b_vn", scr[6], [P, ST, 2 * P])
        b_la = sb("b_la", 72, [P, ST, P])
        b_kdn = sb("b_kdn", 76, [P, ST, P])
        b_r = sb("b_r", 88, [P, 2, S])
        b_vt = sb("b_vt", 136, [P, 2, S])
        b_st = sb("b_st", 144, [P, NCH, P])
        b_att = sb("b_att", 172, [P, S])
        b_v = sb("b_v", 180, [P, S])
        wgu_sb = sb("wgu_sb", 205, [P, 256])
        wgl_raw = sb("wgl_raw", 206, [P, KT * 16])
        wgl_hi = sb("wgl_hi", 206.5, [P, KT, 16], F32R)
        wgl_lo = sb("wgl_lo", 207, [P, KT, 16], F32R)
        a_vt = sb("a_vt", scr[0], [P, S])
        a_vn = [sb("a_vn0", scr[1], [P, ST, P]), sb("a_vn1", 88, [P, ST, P])]
        a_k = [sb("a_k0", scr[2], [P, S]), sb("a_k1", 72, [P, S])]
        a_q = [sb("a_q0", scr[3], [P, S]), sb("a_q1", 76, [P, S])]
        a_sh = sb("a_sh", scr[4], [P, S])
        a_s = sb("a_s", scr[5], [P, 3, S])
        a_pt = sb("a_pt", 172, [P, 2, S])
        a_o = sb("a_o", 180, [P, 2, P])
        pos_i = sb("pos_i", 152, [P, S], I32)
        r_a, r_n, r_r = sb("r_a", 176, [P, S]), sb("r_n", 136, [P, S]), sb("r_r", 140, [P, S])

        ident = cst[:, C_ID:C_ID + P]
        ps = ctx.enter_context(nc.psum_tensor("ps", [P, 8, HALF], F32))

        def slot2(r):
            b = 2 * (r % 4)
            return ps[:, b:b + 2, :].rearrange("p b n -> p (b n)")

        s_cst = sem("constants_loaded")
        s_tab = sem("tables_loaded")
        s_wglr = sem("w_gl_loaded")
        s_cmx = sem("mixer_c_constants_loaded")
        s_x = [sem(f"x_loaded{k}") for k in range(KT)]
        s_wdma = [sem("w_loaded0"), sem("w_loaded1")]
        s_wsplit = sem("w_split")
        s_whi = sem("w_hi_done")
        s_proj = sem("projected")
        s_out = sem("out_stored")
        s_setup = sem("setup_done")

        class Norm:
            def __init__(self, name, col):
                self.col = col
                self.sq = sem(name + "_squared")
                self.acc = sem(name + "_accumulated")
                self.hi = sem(name + "_hi")
                self.lo = sem(name + "_lo")
                self.sum = sem(name + "_summed")
                self.var = sem(name + "_var")
                self.ln = sem(name + "_ln")
                self.exp = sem(name + "_exp")
                self.rstd = sem(name + "_rstd")

        norms = [Norm("norm_a", G_MIX0), Norm("norm_f0", G_FFN0), Norm("norm_c", G_MIX1),
                 Norm("norm_f1", G_FFN1), Norm("norm_out", G_FIN)]

        N_B = 0
        N_A = N_B + 6 * NBP
        N_WO = N_A + 3 * NHP
        N_F0 = N_WO + KT
        FFN_TILES = 3 * FT
        N_V = N_F0 + FFN_TILES
        N_CU = N_V + 8
        N_WOC = N_CU + KT
        N_F1 = N_WOC + KT

        s_wgl = sem("w_gl_split")
        s_fin = sem("final_tile")

        class Bsem:
            def __init__(self):
                self.ready = sem("b_result_ready")
                self.free = sem("b_result_taken")
                self.silu = sem("b_silu")
                self.gl = sem("b_gl_projected")
                self.min = sem("b_min")
                self.e = sem("b_exp_ln")
                self.la = sem("b_log_decay")
                self.dec = sem("b_vector_steps")
                self.state = sem("b_state")
                self.o = sem("b_out_steps")
                self.osq = sem("b_out_act")
        B = Bsem()

        class Asem:
            def __init__(self):
                self.half = sem("a_first_half_projected")
                self.vt = sem("a_v_transposed")
                self.free = sem("a_proj_taken")
                self.vn = sem("a_v_by_position")
                self.rope = sem("a_rope_steps")
                self.k = sem("a_k_ready")
                self.q = sem("a_q_ready")
                self.s = sem("a_scores_ready")
                self.max = sem("a_max_done")
                self.e = sem("a_exp_done")
                self.rl = sem("a_recip_done")
                self.pt = sem("a_transposed")
                self.ptf = sem("a_transposed_taken")
                self.pv = sem("a_pv_done")
                self.o = sem("a_out_scaled")
                self.ot = sem("a_out_transposed")
                self.of = sem("a_out_taken")
        A = Asem()

        class Osem:
            def __init__(self, name):
                self.hi = sem(name + "_hi")
                self.lo = sem(name + "_lo")
                self.added = sem(name + "_added")
        WO, WOC = Osem("wo"), Osem("woc")

        class Fsem:
            def __init__(self, name):
                self.free = sem(name + "_taken")
                self.tap = sem(name + "_taps")
                self.cid = sem(name + "_conv_start")
                self.silu = sem(name + "_silu")
                self.gated = sem(name + "_gated")
                self.ghi = sem(name + "_g_hi")
                self.glo = sem(name + "_g_lo")
        f0, f1 = Fsem("f0"), Fsem("f1")

        class Csem:
            def __init__(self):
                self.slot = sem("c_v_weight_slot_used")
                self.vf = sem("c_v_gelu")
                self.vsq = sem("c_v_squares")
                self.rn = sem("c_rstd_rows")
                self.rnf = sem("c_rstd_rows_taken")
                self.t = sem("c_tiny_steps")
                self.ta = sem("c_tiny_act")
                self.vn = sem("c_v_normed")
                self.ws = sem("c_spatial_masked")
                self.ready = sem("c_result_ready")
                self.free = sem("c_result_taken")
                self.u = sem("c_u_gelu")
                self.gated = sem("c_gated")
        C = Csem()
        s_rope_v = sem("rope_vector_steps")
        s_rope_a = sem("rope_scalar_steps")

        R_A = 6 * NBP
        R_WO = R_A + 3 * NHP
        R_F0 = R_WO + KT
        FFN_RESULTS = 4 * NBLK + KT * NBLK
        R_V = R_F0 + FFN_RESULTS
        R_CU = R_V + 2 * ST
        R_WOC = R_CU + KT
        R_F1 = R_WOC + KT

        block = ctx.enter_context(nc.Block())

        @block.sync
        def _(sp):
            def plain(n, src):
                if n >= 2:
                    sp.wait_ge(s_wsplit, n - 1)
                sp.dma_start(w_raw[:, n % 2, :], src).then_inc(s_wdma[n % 2], 16)

            def looped(base, per, i, t, src):
                sp.wait_ge(s_wsplit, i * per + (base + t - 1))
                sp.dma_start(w_raw[:, (base + t) % 2, :], src).then_inc(s_wdma[(base + t) % 2], 16)

            sp.dma_start(cst[:], consts).then_inc(s_cst, 16)
            sp.dma_start(gain[:], gains).then_inc(s_cst, 16)
            sp.dma_start(cw[:], conv).then_inc(s_cst, 16)
            for k in range(KT):
                sp.dma_start(x[:, k, :], xT[k]).then_inc(s_x[k], 16)
                if k == 1:
                    sp.dma_start(wgl_raw[:], wgl).then_inc(s_wglr, 16)
            sp.dma_start(pos_i[:], pos.partition_broadcast(P)).then_inc(s_tab, 16)
            sp.dma_start(lmul[:], logmul).then_inc(s_tab, 16)
            sp.dma_start(wgu_sb[0:16, :], wgu).then_inc(s_tab, 16)
            sp.dma_start(wgu_sb[16:17, :], bgu).then_inc(s_tab, 16)

            for bp in range(NBP):
                for t, blk in enumerate((KB + bp, QB + bp, VB + 2 * bp, VB + 2 * bp + 1, RB + 2 * bp, RB + 2 * bp + 1)):
                    plain(N_B + 6 * bp + t, w_in[blk])
            for hp in range(NHP):
                for t, blk in enumerate((VA + hp, KA + hp, QA + hp)):
                    plain(N_A + 3 * hp + t, w_in[blk])
            for m in range(KT):
                plain(N_WO + m, w_out[m])

            def ffn(base, layer):
                for t in range(4):
                    plain(base + t, w_up[layer, t])
                with sp.Fori(0, NBLK - 1) as i:
                    for t in range(4):
                        looped(base + 4, 6, i, t, w_up[layer, bass.ds(i * 4 + (4 + t), 1)].rearrange("a p n -> p (a n)"))
                    for t in range(2):
                        looped(base + 4, 6, i, 4 + t, w_dn[layer, bass.ds(i * 2 + t, 1)].rearrange("a p n -> p (a n)"))
                for t in range(2):
                    plain(base + FFN_TILES - 2 + t, w_dn[layer, FT - 2 + t])

            ffn(N_F0, 0)
            for t in range(8):
                plain(N_V + t, w_v[t])
                if t == 0:
                    sp.wait_ge(f0.glo, FT)
                    sp.dma_start(bspb[:], bsp.partition_broadcast(P)).then_inc(s_cmx, 16)
                    sp.dma_start(wst[:], wsT).then_inc(s_cmx, 16)
            for m in range(KT):
                plain(N_CU + m, w_u[m])
            for m in range(KT):
                plain(N_WOC + m, w_outc[m])
            ffn(N_F1, 1)
            for k in range(KT):
                sp.wait_ge(s_fin, k + 1)
                sp.dma_start(outT[k], x[:, k, :]).then_inc(s_out, 16)
            sp.wait_ge(s_out, 16 * KT)

        @block.gpsimd
        def _(pool):
            def split(parity, loaded, slot, done, *free):
                pool.wait_ge(s_wdma[parity], loaded)
                for s_free, count in free:
                    pool.wait_ge(s_free, count)
                pool.tensor_tensor(tiny[:, 62:63], w_raw[:, parity, 0:1], w_raw[:, parity, 0:1], ALU.mult)
                pool.tensor_scalar(w_hi[:, slot, :], w_raw[:, parity, :], 1.0, None, ALU.mult).then_inc(s_whi, 1)
                pool.wait_ge(s_whi, done)
                pool.tensor_tensor(w_lo[:, slot, :], w_raw[:, parity, :], w_hi[:, slot, :].bitcast(F32),
                                   ALU.subtract).then_inc(s_wsplit, 1)

            def plain(n, slot, *free):
                split(n % 2, 16 * (n // 2 + 1), slot, n + 2, *free)

            def looped(n0, i, per, slot, *free):
                split(n0 % 2, i * (8 * per) + 16 * (n0 // 2 + 1), slot, i * per + (n0 + 2), *free)

            pool.wait_ge(s_wglr, 16)
            pool.tensor_scalar(wgl_hi[:], wgl_raw[:], 1.0, None, ALU.mult).then_inc(s_whi, 1)
            pool.wait_ge(s_whi, 1)
            pool.tensor_tensor(wgl_lo[:], wgl_raw[:], wgl_hi[:].bitcast(F32), ALU.subtract).then_inc(s_wgl, 1)
            plain(0, 0)
            plain(1, 1)
            with pool.Fori(0, (N_F0 - 2) // 2) as i:
                for t in range(2):
                    looped(2 + t, i, 2, t, (s_proj, i * 2 + (t + 1)))

            def ffn(base, res):
                for t in range(4):
                    plain(base + t, t, (s_proj, res - 1 if t == 0 else res))
                with pool.Fori(0, NBLK - 1) as i:
                    for t in range(4):
                        looped(base + 4 + t, i, 6, t % 2, (s_proj, i * 12 + (res + t + (1 if t < 2 else 3))))
                    for t in range(2):
                        looped(base + 8 + t, i, 6, 2 + t, (s_proj, i * 12 + (res + 4)))
                for t in range(2):
                    plain(base + FFN_TILES - 2 + t, 2 + t, (s_proj, res + FFN_RESULTS - KT))

            ffn(N_F0, R_F0)
            for t in range(4):
                plain(N_V + t, t, (s_proj, R_V - KT if t < 2 else R_V))
            for t in range(4):
                plain(N_V + 4 + t, t, (C.slot, t + 1) if t < 3 else (s_proj, R_V + ST))
            for m in range(KT):
                plain(N_CU + m, m % 2, (C.slot, 4 + m) if m < 2 else (s_proj, R_CU + m - 1))
            plain(N_WOC, 0, (s_proj, R_WOC - 1))
            plain(N_WOC + 1, 1, (s_proj, R_WOC))
            with pool.Fori(0, (KT - 2) // 2) as i:
                for t in range(2):
                    looped(N_WOC + 2 + t, i, 2, t, (s_proj, i * 2 + (R_WOC + t + 1)))
            ffn(N_F1, R_F1)

        def kv_col(c):
            return (c % 2) * HALF + (c // 2) * 256

        UNITS = 16 * NHP
        V0, V1, T0, T1, K0, Q0, K1, Q1 = range(8)

        def unit(U):
            return U // 16, U % 16 // 2, U % 2

        def groups(qt):
            return range(0, qt + 1, 4)

        def groups_before(U):
            return sum(len(groups(unit(v)[1])) for v in range(U))

        PIECES = (5, 4, 4, 3, 3, 2, 2, 2)

        def part_step(part):
            last = (7, 15, 16, 17, 25, 33, 41, 49)[part]
            total = 0
            for u in range(16):
                total += PIECES[u // 2]
                if last < total:
                    return u

        WO_ORDER = (4, 5, 6, 7, 0, 1, 2, 3)

        @block.tensor
        def _(pe):
            def cross(out_of, act_hi_k, act_lo_k, wh, wl, k, first, last):
                out = out_of
                ins = None
                for h in range(2):
                    cols = slice(h * HALF, (h + 1) * HALF)
                    pe.matmul(out[:, cols], wh, act_hi_k[:, cols], start=first, stop=False)
                for h in range(2):
                    cols = slice(h * HALF, (h + 1) * HALF)
                    pe.matmul(out[:, cols], wh, act_lo_k[:, cols], start=False, stop=False)
                for h in range(2):
                    cols = slice(h * HALF, (h + 1) * HALF)
                    ins = pe.matmul(out[:, cols], wl, act_hi_k[:, cols], start=False, stop=last)
                return ins

            def project(out, slot, split_done, lo_sem=None):
                pe.wait_ge(s_wsplit, split_done)
                for k in range(KT):
                    if lo_sem is not None:
                        pe.wait_ge(lo_sem, k + 1)
                    ins = cross(out, act_hi[:, k, :], act_lo[:, k, :], w_hi[:, slot, k * P:(k + 1) * P],
                                w_lo[:, slot, k * P:(k + 1) * P], k, k == 0, k == KT - 1)
                ins.then_inc(s_proj, 1)

            def sum_squares(norm, out):
                pe.wait_ge(norm.acc, KT)
                for h in range(2):
                    ins = pe.matmul(out[:, h * HALF:(h + 1) * HALF], ones[:], acc[:, h * HALF:(h + 1) * HALF],
                                    start=True, stop=True)
                ins.then_inc(norm.sum, 1)

            pe.wait_ge(s_wgl, 1)
            out = ps[0:16, 0:2, :].rearrange("p b n -> p (b n)")
            for k in range(KT):
                pe.wait_ge(norms[0].lo, k + 1)
                ins = cross(out, act_hi[:, k, :], act_lo[:, k, :], wgl_hi[:, k, :], wgl_lo[:, k, :], k, k == 0, k == KT - 1)
            ins.then_inc(B.gl, 1)
            pe.wait_ge(s_setup, 1)
            sum_squares(norms[0], slot2(1))

            with pe.Fori(0, NBP) as i:
                def need(r):
                    if r == 0:
                        pe.wait_ge(B.free, i * 15 + 1)
                    elif 4 <= r < 14:
                        pe.wait_ge(B.free, i * 15 + (r - 2))
                    elif 14 <= r < 18:
                        pe.wait_ge(B.state, i * 31 + min(8 * (r - 13) + 1, 31))
                    elif r >= 18:
                        pe.wait_ge(B.free, i * 15 + (r - 6))

                def proj(r, t):
                    need(r)
                    project(slot2(r), t % 2, i * 6 + (N_B + t + 1))

                pe.wait_ge(norms[0].var, 1)
                proj(0, 0)
                proj(1, 1)
                need(2)
                pe.wait_ge(B.free, 1)
                pe.wait_ge(s_tab, 16 * 4)
                for st in range(ST):
                    ins = pe.matmul(slot2(2)[:, st * P:(st + 1) * P], glT[0:17, st * P:(st + 1) * P],
                                    wgu_sb[0:17, bass.ts(i, P)], start=True, stop=True)
                ins.then_inc(B.ready, 1)
                proj(3, 2)
                need(4)
                pe.wait_ge(B.la, i + 1)
                for st in range(ST):
                    ins = pe.matmul(slot2(4)[:, st * P:(st + 1) * P], b_la[:, st, :], cst[:, C_U:C_U + P],
                                    start=True, stop=True)
                ins.then_inc(B.ready, 1)
                proj(5, 3)
                need(6)
                pe.wait_ge(B.dec, i * 6 + 2)
                for st in range(ST):
                    ins = pe.transpose(slot2(6)[:, st * P:(st + 1) * P], b_kd[:, st * P:(st + 1) * P], ident)
                ins.then_inc(B.ready, 1)
                for h in range(2):
                    need(7 + h)
                    pe.wait_ge(B.free, i * 15 + (1 + (4 if h == 0 else 6)))
                    for st in range(ST):
                        ins = pe.transpose(slot2(7 + h)[:, st * P:(st + 1) * P], b_vt[:, h, st * P:(st + 1) * P], ident)
                    ins.then_inc(B.ready, 1)
                proj(9, 4)
                pe.wait_ge(B.free, i * 15 + 10)
                for g in range(4):
                    need(10 + g)
                    for c in range(4):
                        n = 4 * g + c
                        rows = slice(CH * (n % 2), CH * (n % 2) + CH)
                        col = kv_col(c)
                        ins = pe.matmul(slot2(10 + g)[:, col:col + 256], b_kdn[rows, n // 2, :],
                                        b_vn[rows, n // 2, :], start=True, stop=True)
                    ins.then_inc(B.ready, 1)
                proj(14, 5)
                pe.wait_ge(B.dec, i * 6 + 6)
                for h in range(2):
                    need(15 + h)
                    rows = slice(64 * h, 64 * h + 64)
                    for st in range(ST):
                        cols = slice(st * P, (st + 1) * P)
                        ins = pe.matmul(slot2(15 + h)[:, cols], b_k[rows, cols], b_q[rows, cols], start=True, stop=True)
                    ins.then_inc(B.ready, 1)
                pe.wait_ge(B.state, i * 31 + 31)
                for h in range(2):
                    need(17 + h)
                    pe.wait_ge(B.free, i * 15 + (13 + h))
                    rows = slice(64 * h, 64 * h + 64)
                    out = slot2(17 + h)
                    att = b_att if h == 0 else b_cum
                    for st in range(ST):
                        pe.matmul(out[:, st * P:(st + 1) * P], b_vn[:, st, h * P:(h + 1) * P], att[:, st * P:(st + 1) * P],
                                  start=True, stop=True, skip_group_check=True)
                        for n in (2 * st, 2 * st + 1):
                            ins = pe.matmul(out[:, n * CH:(n + 1) * CH], b_st[rows, n, :], b_qe[rows, n * CH:(n + 1) * CH],
                                            start=False, stop=True, skip_group_check=True)
                    ins.then_inc(B.ready, 1)
                for h in range(2):
                    need(19 + h)
                    pe.wait_ge(B.osq, i * 6 + 3 * h + 1)
                    for c in range(2):
                        ins = pe.matmul(slot2(19 + h)[:, c * HALF:(c + 1) * HALF], ones[:], b_v[:, c * HALF:(c + 1) * HALF],
                                        start=True, stop=True)
                    ins.then_inc(B.ready, 1)
                pe.wait_ge(B.o, i * 14 + 9)

            pe.wait_ge(B.free, 15 * NBP + 1)

            def half_tile(hp, t, h, bank, k):
                n = N_A + 3 * hp + t
                if k == 0:
                    pe.wait_ge(s_wsplit, n + 1)
                out, cols, wcols = ps[:, bank, :], slice(h * HALF, (h + 1) * HALF), slice(k * P, (k + 1) * P)
                pe.matmul(out, w_hi[:, n % 2, wcols], act_hi[:, k, cols], start=(k == 0), stop=False)
                pe.matmul(out, w_hi[:, n % 2, wcols], act_lo[:, k, cols], start=False, stop=False)
                ins = pe.matmul(out, w_lo[:, n % 2, wcols], act_hi[:, k, cols], start=False, stop=(k == KT - 1))
                if k == KT - 1:
                    ins.then_inc(A.half if h == 0 else s_proj, 1)

            def v_transposes(hp, h):
                pe.wait_ge(A.free, 6 * hp + 1 + h)
                for st in range(4 * h, 4 * h + 4):
                    ins = pe.transpose(ps[:, h, (st % 4) * P:(st % 4 + 1) * P], a_vt[:, st * P:(st + 1) * P], ident)
                ins.then_inc(A.vt, 1)

            def piece(hp, j):
                if j < 16:
                    part, k = j // 8, j % 8
                elif j < 18:
                    part, k = T0 + j - 16, 0
                else:
                    part, k = K0 + (j - 18) // 8, (j - 18) % 8
                if part == V0 or part == V1:
                    if k == 0 and hp:
                        pe.wait_ge(A.free, 6 * hp - 1 + part)
                    half_tile(hp, 0, part, part, k)
                elif part == T0 or part == T1:
                    v_transposes(hp, part - T0)
                elif part == K0 or part == Q0:
                    if k == 0:
                        pe.wait_ge(A.vn, 2 * hp + 1 + part - K0)
                    half_tile(hp, 1 + part - K0, 0, part - K0, k)
                else:
                    if k == 0:
                        pe.wait_ge(A.free, 6 * hp + 3 + part - K1)
                    half_tile(hp, 1 + part - K1, 1, part - K1, k)

            def wo_piece(m, j):
                kk, h = j // 2, j % 2
                k, n = WO_ORDER[kk], N_WO + m
                if j == 0:
                    pe.wait_ge(s_wsplit, n + 1)
                pe.wait_ge(WO.lo, kk + 1)
                out, cols, wcols = ps[:, 2 * m + h, :], slice(h * HALF, (h + 1) * HALF), slice(k * P, (k + 1) * P)
                pe.matmul(out, w_hi[:, n % 2, wcols], act_hi[:, k, cols], start=(kk == 0), stop=False)
                pe.matmul(out, w_hi[:, n % 2, wcols], act_lo[:, k, cols], start=False, stop=False)
                ins = pe.matmul(out, w_lo[:, n % 2, wcols], act_hi[:, k, cols], start=False, stop=(kk == KT - 1))
                if j == 2 * KT - 1:
                    ins.then_inc(s_proj, 1)

            def fill(U, part, parts):
                hp, qt, h = unit(U)
                if hp < NHP - 1:
                    n = PIECES[qt]
                    first = sum(PIECES[unit(v)[1]] for v in range(16 * hp, U))
                    for j in range(n * part // parts, n * (part + 1) // parts):
                        piece(hp + 1, first + j)
                elif 4 <= U % 16 < 11:
                    for j in range(2 * part // parts, 2 * (part + 1) // parts):
                        wo_piece(0, 2 * (U % 16 - 4) + j)

            def scores(U):
                hp, qt, h = unit(U)
                keys = (qt + 1) * P
                pe.wait_ge(A.k, 2 * hp + (1 if qt < 4 else 2))
                pe.wait_ge(A.q, 2 * hp + (1 if qt < 4 else 2))
                if U >= 2:
                    pe.wait_ge(A.max, U - 1)
                rows, out = slice(64 * h, 64 * h + 64), slot2(1 + U % 2)
                for c in range(0, keys, HALF):
                    n = min(HALF, keys - c)
                    ins = pe.matmul(out[:, c:c + n], a_q[hp % 2][rows, qt * P:(qt + 1) * P], a_k[hp % 2][rows, c:c + n],
                                    start=True, stop=True)
                ins.then_inc(A.s, 1)

            def transposes(U, gi):
                qt = unit(U)[1]
                g = groups_before(U) + gi
                pe.wait_ge(A.e, U + 1)
                if g:
                    pe.wait_ge(A.ptf, g)
                for kt in range(4 * gi, min(4 * gi + 4, qt + 1)):
                    ins = pe.transpose(ps[:, 6, (kt % 4) * P:(kt % 4 + 1) * P], a_s[:, U % 3, kt * P:(kt + 1) * P], ident)
                ins.then_inc(A.pt, 1)

            def values(U):
                hp, qt, h = unit(U)
                pe.wait_ge(A.ptf, groups_before(U + 1))
                if U >= 1:
                    pe.wait_ge(A.o, U)
                if U >= 2:
                    pe.wait_ge(A.of, U // 2)
                for kt in range(qt + 1):
                    ins = pe.matmul(ps[:, 7, (U % 4) * 64:(U % 4 + 1) * 64], a_pt[:, U % 2, kt * P:(kt + 1) * P],
                                    a_vn[hp % 2][:, kt, 64 * h:64 * h + 64], start=(kt == 0), stop=(kt == qt))
                ins.then_inc(A.pv, 1)

            def out_transpose(n):
                pe.wait_ge(A.o, 2 * n + 2)
                pe.transpose(ps[:, 7, 256 + (n % 2) * P:256 + (n % 2 + 1) * P], a_o[:, n % 2, :], ident).then_inc(A.ot, 1)

            for j in range(42):
                piece(0, j)
            scores(0)
            scores(1)
            for j in range(42, 50):
                piece(0, j)
            for U in range(UNITS):
                if U + 2 < UNITS:
                    scores(U + 2)
                if U % 2 and U >= 3:
                    out_transpose((U - 3) // 2)
                fill(U, 0, 3)
                transposes(U, 0)
                fill(U, 1, 3)
                if U:
                    values(U - 1)
                if len(groups(unit(U)[1])) == 2:
                    transposes(U, 1)
                fill(U, 2, 3)
            pe.wait_ge(A.max, UNITS)
            for j in range(2):
                wo_piece(1, j)
            values(UNITS - 1)
            for j in range(2, 4):
                wo_piece(1, j)
            out_transpose(UNITS // 2 - 1)
            for j in range(4, 14):
                wo_piece(1, j)
            for m in range(2):
                for j in range(14, 16):
                    wo_piece(m, j)

            def residual(O, base, first):
                for m in range(first, KT):
                    if m >= 4:
                        pe.wait_ge(O.added, m - 3)
                    project(slot2(m), (base + m) % 2, base + m + 1, O.lo if m == 0 else None)

            pe.wait_ge(A.of, UNITS // 2)
            residual(WO, N_WO, 2)

            def ffn(F, base, norm, prev):
                pe.wait_ge(prev.added, KT)

                def up(r, t, slot, split_done, lo_sem=None):
                    project(slot2(r), slot, split_done, lo_sem)

                def down(r0, par, ready_g, split_done, waits):
                    pe.wait_ge(F.glo, ready_g)
                    pe.wait_ge(s_wsplit, split_done)
                    for m in range(KT):
                        waits(r0 + m)
                        out = slot2(r0 + m)
                        for t in range(2):
                            ins = cross(out, g_hi[:, 2 * par + t, :], g_lo[:, 2 * par + t, :],
                                        w_hi[:, 2 + t, m * P:(m + 1) * P], w_lo[:, 2 + t, m * P:(m + 1) * P],
                                        m, t == 0, t == 1)
                        ins.then_inc(s_proj, 1)

                up(0, 0, 0, base + 1, norm.lo)
                sum_squares(norm, slot2(1))
                for t in range(1, 4):
                    if t == 3:
                        pe.wait_ge(F.free, 1)
                    up(t + 1, t, t, base + t + 1)
                with pe.Fori(0, (NBLK - 1) // 2) as i:
                    pe.wait_ge(norm.var, 1)
                    for par in range(2):
                        for t in range(4):
                            n = 4 + 12 * par + t
                            pe.wait_ge(F.free, i * 24 + (n - 3))
                            up(n + 1, t, t % 2, i * 12 + (base + 4 + 6 * par + t + 1))
                        down(4 + 12 * par + 4 + 1, par, i * 4 + (2 * par + 2), i * 12 + (base + 4 + 6 * par + 6),
                             lambda r: pe.wait_ge(F.free, i * 24 + (r - 4)))
                last = 4 + 12 * (NBLK - 1)
                down(last + 1, 0, FT, base + FFN_TILES, lambda r: pe.wait_ge(F.free, r - 4))

            ffn(f0, N_F0, norms[1], WO)
            F_TOTAL = 4 + 12 * (NBLK - 1) + 8
            pe.wait_ge(f0.free, F_TOTAL)

            def v_tile(half, st):
                n = 8 * half + st
                bank = n % 6
                if n >= 6:
                    pe.wait_ge(C.vf, n - 5)
                out = ps[:, bank, :]
                for k in range(KT):
                    slot, kk = k // 2, k % 2
                    if st == 0:
                        pe.wait_ge(s_wsplit, N_V + 4 * half + slot + 1)
                    if n == 0:
                        pe.wait_ge(norms[2].lo, k + 1)
                    cols = slice(kk * HALF, (kk + 1) * HALF)
                    pcols = slice(st * P, (st + 1) * P)
                    pe.matmul(out, act_hi[:, k, pcols], w_hi[:, slot, cols], start=(k == 0), stop=False)
                    pe.matmul(out, act_hi[:, k, pcols], w_lo[:, slot, cols], start=False, stop=False)
                    ins = pe.matmul(out, act_lo[:, k, pcols], w_hi[:, slot, cols], start=False, stop=(k == KT - 1))
                    if k == KT - 1:
                        ins.then_inc(s_proj, 1)
                    elif st == ST - 1 and kk == 1:
                        ins.then_inc(C.slot, 1)

            v_tile(0, 0)
            sum_squares(norms[2], slot2(3))
            v_tile(0, 1)
            v_tile(0, 2)
            v_tile(0, 3)
            pe.wait_ge(norms[2].rstd, 1)
            for st in range(ST):
                ins = pe.matmul(ps[:, 7, st:st + 1], rstd[0:1, st * P:(st + 1) * P], ones[0:1, 0:1], start=True, stop=True)
            ins.then_inc(C.rn, 1)
            for n in range(4, 16):
                v_tile(n // 8, n % 8)

            def c_u(r, m):
                if r >= 4:
                    pe.wait_ge(C.free, r - 3)
                project(slot2(r), (N_CU + m) % 2, N_CU + m + 1)

            pe.wait_ge(C.vf, 16)
            c_u(0, 0)
            c_u(1, 1)
            pe.wait_ge(C.rnf, 1)
            pe.wait_ge(C.ws, 1)
            pe.wait_ge(C.vn, ST)
            for g in range(KT):
                r = 2 + g
                if r >= 4:
                    pe.wait_ge(C.free, r - 3)
                for n in range(ST):
                    ins = pe.matmul(slot2(r)[:, n * P:(n + 1) * P], vs[:, g, n, :], wst[:, g, :], start=True, stop=True)
                ins.then_inc(C.ready, 1)
            for m in range(2, KT):
                c_u(8 + m, m)

            pe.wait_ge(C.free, 16)
            residual(WOC, N_WOC, 0)
            ffn(f1, N_F1, norms[3], WOC)
            pe.wait_ge(f1.free, F_TOTAL)
            sum_squares(norms[4], slot2(0))

        @block.vector
        def _(dve):
            def carry_wait(j):
                dve.memset(carry[:, j:j + 1], 0.0)

            def norm_rstd(norm, psum):
                dve.wait_ge(norm.sum, 1)
                v, t = sq[:, 0, :], sq[:, 1, :]
                dve.tensor_scalar(v, psum, 1.0 / D, EPS, ALU.mult, ALU.add).then_inc(norm.var, 1)
                dve.wait_ge(norm.exp, 1)
                dve.scalar_tensor_tensor(t, v, -0.5, rstd[:], ALU.mult, ALU.mult).then_inc(norm.var, 1)
                dve.wait_ge(norm.var, 2)
                dve.tensor_tensor(v, t, rstd[:], ALU.mult).then_inc(norm.var, 1)
                dve.wait_ge(norm.var, 3)
                dve.scalar_tensor_tensor(rstd[:], v, 1.5, rstd[:], ALU.add, ALU.mult).then_inc(norm.rstd, 1)

            def accumulate(norm, k):
                dve.wait_ge(norm.sq, k + 1)
                if k:
                    dve.wait_ge(norm.acc, k)
                if k == 0:
                    dve.tensor_copy(acc[:], sq[:, 0, :]).then_inc(norm.acc, 1)
                else:
                    dve.tensor_tensor(acc[:], acc[:], sq[:, k % 2, :], ALU.add).then_inc(norm.acc, 1)

            def act_low(norm, k):
                dve.wait_ge(norm.hi, k + 1)
                dve.scalar_tensor_tensor(act_lo[:, k, :], x[:, k, :], gain[:, norm.col + k:norm.col + k + 1],
                                         act_hi[:, k, :].bitcast(F32), ALU.mult, ALU.subtract).then_inc(norm.lo, 1)

            dve.memset(ones[:], 1.0).then_inc(s_setup, 1)
            dve.memset(glT[0:32, :], 1.0).then_inc(s_rope_v, 1)
            for k in range(KT):
                act_low(norms[0], k)
                accumulate(norms[0], k)
            norm_rstd(norms[0], slot2(1))

            dve.wait_ge(B.gl, 1)
            dve.wait_ge(norms[0].rstd, 1)
            dve.wait_ge(s_rope_v, 1)
            dve.tensor_tensor(glT[0:16, :], ps[0:16, 0:2, :].rearrange("p b n -> p (b n)"), rstd[0:16, :],
                              ALU.mult).then_inc(B.free, 1)

            n_v = [1]

            def step(ins):
                ins.then_inc(s_rope_v, 1)
                n_v[0] += 1
                dve.wait_ge(s_rope_v, n_v[0])

            dve.wait_ge(s_tab, 16 * 4)
            step(dve.tensor_copy(r_a[:], pos_i[:]))
            step(dve.tensor_scalar(r_a[:], r_a[:], cst[:, C_INV:C_INV + 1], None, ALU.mult))
            step(dve.tensor_scalar(r_n[:], r_a[:], 1.0 / TWO_PI, MAGIC, ALU.mult, ALU.add))
            step(dve.tensor_scalar(r_n[:], r_n[:], -MAGIC, None, ALU.add))
            for part in PI_PARTS:
                step(dve.scalar_tensor_tensor(r_a[:], r_n[:], -part, r_a[:], ALU.mult, ALU.add))
            step(dve.tensor_scalar(r_a[:], r_a[:], 3.1415925, -3.1415925, ALU.min, ALU.max))
            dve.wait_ge(s_rope_a, 2)
            step(dve.scalar_tensor_tensor(ropeC[:], r_r[:], -2.0, r_r[:], ALU.mult, ALU.mult))
            dve.scalar_tensor_tensor(ropeC[:], ropeC[:], 1.0, rstd[:], ALU.add, ALU.mult).then_inc(s_rope_v, 1)
            dve.scalar_tensor_tensor(ropeS[:], ropeS[:], cst[:, C_SGN:C_SGN + 1], rstd[:], ALU.mult,
                                     ALU.mult).then_inc(s_rope_v, 1)
            n_v[0] += 2
            rope_done = n_v[0]

            with dve.Fori(0, NBP) as i:
                weights = (0, 1, 3, 5, 9, 14)

                def ready(r):
                    if r in weights:
                        dve.wait_ge(s_proj, i * 6 + (weights.index(r) + 1))
                    else:
                        dve.wait_ge(B.ready, i * 15 + (r + 1 - sum(w < r for w in weights)))

                def chunks(t):
                    return t.rearrange("p (n c) -> p n c", c=CH)

                def at(t, c):
                    return chunks(t)[:, :, c:c + 1].to_broadcast([P, NCH, CH])

                ready(0)
                dve.tensor_tensor(b_k[:], slot2(0), rstd[:], ALU.mult).then_inc(B.free, 1)
                ready(1)
                dve.tensor_tensor(b_q[:], slot2(1), rstd[:], ALU.mult).then_inc(B.free, 1)
                ready(2)
                dve.tensor_scalar(b_cum[:], slot2(2), 0.0, None, ALU.min).then_inc(B.min, 1)
                dve.wait_ge(B.min, i + 1)
                dve.scalar_tensor_tensor(b_e[:], b_cum[:], 2.0, slot2(2), ALU.mult, ALU.subtract).then_inc(B.free, 1)
                dve.wait_ge(B.e, i * 6 + 2)
                dve.wait_ge(B.free, i * 15 + 4)
                dve.tensor_tensor(b_la[:].rearrange("p a b -> p (a b)"), b_cum[:], b_e[:], ALU.subtract).then_inc(B.la, 1)
                ready(3)
                dve.tensor_tensor(b_vt[:, 0, :], slot2(3), rstd[:], ALU.mult).then_inc(B.free, 1)
                ready(4)
                dve.tensor_copy(b_cum[:], slot2(4)).then_inc(B.free, 1)
                dve.wait_ge(B.free, i * 15 + 6)
                dve.tensor_tensor(chunks(b_e[:]), at(b_cum[:], CH - 1), chunks(b_cum[:]), ALU.subtract).then_inc(B.dec, 1)
                dve.wait_ge(B.e, i * 6 + 3)
                dve.tensor_tensor(b_kd[:], b_k[:], b_e[:], ALU.mult).then_inc(B.dec, 1)
                ready(5)
                dve.tensor_tensor(b_vt[:, 1, :], slot2(5), rstd[:], ALU.mult).then_inc(B.free, 1)
                dve.wait_ge(B.dec, i * 6 + 2)
                dve.tensor_tensor(chunks(b_e[:]), chunks(b_cum[:]), at(b_cum[:], CH // 2 - 1), ALU.subtract).then_inc(B.dec, 1)
                dve.wait_ge(B.e, i * 6 + 6)
                dve.scalar_tensor_tensor(b_qe[:], b_q[:], A_SCALE, b_cum[:], ALU.mult, ALU.mult).then_inc(B.dec, 1)
                dve.scalar_tensor_tensor(b_q[:], b_q[:], A_SCALE, b_v[:], ALU.mult, ALU.mult).then_inc(B.dec, 1)
                dve.tensor_tensor(b_k[:], b_k[:], b_e[:], ALU.mult).then_inc(B.dec, 1)
                ready(6)
                dve.tensor_copy(b_kdn[:].rearrange("p a b -> p (a b)"), slot2(6)).then_inc(B.free, 1)
                for h in range(2):
                    ready(7 + h)
                    dve.tensor_copy(b_vn[:, :, h * P:(h + 1) * P], slot2(7 + h).rearrange("p (a b) -> p a b", b=P)
                                    ).then_inc(B.free, 1)
                ready(9)
                dve.tensor_tensor(b_r[:, 0, :], slot2(9), rstd[:], ALU.mult).then_inc(B.free, 1)
                dve.memset(b_st[:, 0, :], 0.0).then_inc(B.state, 1)
                dve.memset(b_att[:], 0.0).then_inc(B.o, 1)
                for g in range(4):
                    ready(10 + g)
                    kv = slot2(10 + g)
                    for c in range(4):
                        n = 4 * g + c
                        if n == NCH - 1:
                            break
                        dve.wait_ge(B.state, i * 31 + (2 * n + 1))
                        for h in range(2):
                            rows = slice(64 * h, 64 * h + 64)
                            ins = dve.scalar_tensor_tensor(
                                b_st[rows, n + 1, :], b_st[rows, n, :], b_cum[rows, n * CH + CH - 1:(n + 1) * CH],
                                kv[rows, kv_col(c) + h * P:kv_col(c) + (h + 1) * P], ALU.mult, ALU.add)
                            ins.then_inc(B.state, 1)
                ready(14)
                dve.tensor_tensor(b_r[:, 1, :], slot2(14), rstd[:], ALU.mult).then_inc(B.free, 1)
                mask = cst[:, C_M64:C_M64 + P].bitcast(U32)
                dve.wait_ge(B.state, i * 31 + 31)
                dve.memset(b_cum[:], 0.0).then_inc(B.o, 1)
                dve.wait_ge(B.o, i * 14 + 2)
                for h in range(2):
                    ready(15 + h)
                    carry_wait(h)
                    att = b_att if h == 0 else b_cum
                    for c in range(ST):
                        ins = dve.copy_predicated(att[:, c * P:(c + 1) * P], mask, slot2(15 + h)[:, c * P:(c + 1) * P])
                    ins.then_inc(B.free, 1)
                for h in range(2):
                    ready(17 + h)
                    dve.tensor_copy(b_k[:] if h == 0 else b_q[:], slot2(17 + h)).then_inc(B.free, 1)
                for h in range(2):
                    o = b_k if h == 0 else b_q
                    v, y, t = b_e, b_kd, b_qe
                    c0 = i * 14 + (2 + 6 * h)
                    ready(19 + h)
                    dve.tensor_scalar(v[:], slot2(19 + h), 1.0 / P, EPS, ALU.mult, ALU.add).then_inc(B.o, 1)
                    dve.wait_ge(B.osq, i * 6 + (3 * h + 3))
                    dve.scalar_tensor_tensor(t[:], v[:], -0.5, y[:], ALU.mult, ALU.mult).then_inc(B.o, 1)
                    dve.wait_ge(B.o, c0 + 2)
                    dve.tensor_tensor(t[:], t[:], y[:], ALU.mult).then_inc(B.o, 1)
                    dve.wait_ge(B.o, c0 + 3)
                    dve.scalar_tensor_tensor(y[:], t[:], 1.5, y[:], ALU.add, ALU.mult).then_inc(B.o, 1)
                    dve.wait_ge(B.o, c0 + 4)
                    dve.scalar_tensor_tensor(t[:], o[:], gain[:, G_OUT:G_OUT + 1], y[:], ALU.mult, ALU.mult).then_inc(B.o, 1)
                    dve.wait_ge(B.o, c0 + 5)
                    dve.wait_ge(B.silu, i * 2 + (h + 1))
                    dve.tensor_tensor(oT[:, bass.ds(i * 2 + (4 + h), 1), :].rearrange("p a n -> p (a n)"), t[:],
                                      b_r[:, h, :], ALU.mult).then_inc(B.o, 1)

            dve.wait_ge(s_rope_v, rope_done)

            def take_v(hp, h):
                cols = slice(h * HALF, (h + 1) * HALF)
                if h == 0:
                    dve.wait_ge(A.half, 3 * hp + 1)
                    if hp:
                        dve.wait_ge(A.vn, 2 * hp)
                else:
                    dve.wait_ge(s_proj, R_A + 3 * hp + 1)
                dve.tensor_tensor(a_vt[:, cols], ps[:, h, :], rstd[:, cols], ALU.mult).then_inc(A.free, 1)

            def rope(hp, is_q, h):
                cols, n = slice(h * HALF, (h + 1) * HALF), 4 * hp + 2 * h + is_q
                psum, out, sh = ps[:, is_q, :], (a_q if is_q else a_k)[hp % 2][:, cols], a_sh[:, is_q * HALF:(is_q + 1) * HALF]
                if h == 0:
                    dve.wait_ge(A.half, 3 * hp + 2 + is_q)
                else:
                    dve.wait_ge(s_proj, R_A + 3 * hp + 2 + is_q)
                dve.stream_shuffle(sh, psum, [(j + 8) % 16 if j < 16 else j for j in range(32)]).then_inc(A.rope, 1)
                dve.tensor_tensor(out, psum, ropeC[:, cols], ALU.mult).then_inc(A.free, 1)
                dve.wait_ge(A.rope, 2 * n + 1)
                dve.tensor_tensor(sh, sh, ropeS[:, cols], ALU.mult).then_inc(A.rope, 1)
                dve.wait_ge(A.free, 6 * hp + 3 + 2 * h + is_q)
                dve.wait_ge(A.rope, 2 * n + 2)
                dve.tensor_tensor(out, out, sh, ALU.add).then_inc(A.q if is_q else A.k, 1)

            def top(U):
                keys = (unit(U)[1] + 1) * P
                dve.wait_ge(A.s, U + 1)
                if U >= 3:
                    dve.wait_ge(A.pt, groups_before(U - 2))
                if U >= 4:
                    dve.wait_ge(A.e, U - 3)
                dve.tensor_tensor_reduce(a_s[:, U % 3, 0:keys], slot2(1 + U % 2)[:, 0:keys], lmul[:, S - keys:S],
                                         -A_SCALE, 1e30, ALU.add, ALU.min, tiny[:, 8 + U % 4:9 + U % 4]).then_inc(A.max, 1)

            def take_out(U):
                n, h = U // 2, U % 2
                dve.wait_ge(A.e, U + 1)
                rl = tiny[:, 16 + U % 4:17 + U % 4]
                dve.reciprocal(rl, tiny[:, 12 + U % 4:13 + U % 4]).then_inc(A.rl, 1)
                dve.wait_ge(A.rl, U + 1)
                dve.wait_ge(A.pv, U + 1)
                if n >= 2:
                    dve.wait_ge(A.ot, n - 1)
                dve.tensor_scalar(a_o[:, n % 2, 64 * h:64 * h + 64], ps[:, 7, (U % 4) * 64:(U % 4 + 1) * 64], rl, None,
                                  ALU.mult).then_inc(A.o, 1)

            def take_transposed(n):
                dve.wait_ge(A.ot, n + 1)
                qt = n % ST
                dve.tensor_copy(oT[:, n // ST, qt * P:(qt + 1) * P], ps[:, 7, 256 + (n % 2) * P:256 + (n % 2 + 1) * P]
                                ).then_inc(A.of, 1)

            def take_part(hp, part):
                if part < 2:
                    take_v(hp, part)
                elif part >= K0:
                    rope(hp, (part - K0) % 2, (part - K0) // 2)

            def split_low(O, j, k):
                dve.wait_ge(O.hi, j + 1)
                t = oT[:, k, :] if O is WO else vs[:, k, :, :].rearrange("p a b -> p (a b)")
                dve.tensor_tensor(act_lo[:, k, :], t, act_hi[:, k, :].bitcast(F32), ALU.subtract).then_inc(O.lo, 1)

            for part in (V0, V1, K0, Q0):
                take_part(0, part)
            top(0)
            take_part(0, K1)
            top(1)
            take_part(0, Q1)
            for U in range(UNITS):
                hp, u = U // 16, U % 16
                if U + 2 < UNITS:
                    top(U + 2)
                if U % 2 and U >= 3:
                    take_transposed((U - 3) // 2)
                if hp < NHP - 1:
                    for part in range(8):
                        if part_step(part) == u:
                            take_part(hp + 1, part)
                elif 2 <= u < 9:
                    split_low(WO, u - 2, WO_ORDER[u - 2])
                if U:
                    take_out(U - 1)
            take_out(UNITS - 1)
            take_transposed(UNITS // 2 - 1)
            split_low(WO, KT - 1, NHP - 1)

            def residual(O, res, norm, reload):
                if O is not WO:
                    for k in range(KT):
                        split_low(O, k, k)
                for m in range(KT):
                    if reload:
                        dve.wait_ge(s_x[m], 32)
                    dve.wait_ge(s_proj, res + m + 1)
                    dve.tensor_tensor(x[:, m, :], x[:, m, :], slot2(m), ALU.add).then_inc(O.added, 1)
                    if 1 <= m < KT - 1:
                        accumulate(norm, m - 1)
                act_low(norm, 0)
                act_low(norm, 1)
                accumulate(norm, KT - 2)
                act_low(norm, 2)
                accumulate(norm, KT - 1)
                for k in range(3, KT):
                    act_low(norm, k)

            residual(WO, R_WO, norms[1], True)

            def ffn(F, layer, res, norm, nxt, last):
                def up(n, r_slot, g):
                    dve.wait_ge(s_proj, n)
                    dve.tensor_tensor(fz[:, g, :], slot2(r_slot), rstd[:], ALU.mult).then_inc(F.free, 1)

                def taps(g, cid, tap0, tile):
                    dve.wait_ge(F.cid, cid)
                    c1 = cw[:, layer, bass.ds(tile, 1), 1:2].rearrange("p a b -> p (a b)")
                    c0 = cw[:, layer, bass.ds(tile, 1), 0:1].rearrange("p a b -> p (a b)")
                    dve.scalar_tensor_tensor(fc[:, g, 1:S], fz[:, g, 0:S - 1], c1, fc[:, g, 1:S],
                                             ALU.mult, ALU.add).then_inc(F.tap, 1)
                    dve.wait_ge(F.tap, tap0 + 1)
                    dve.scalar_tensor_tensor(fc[:, g, 2:S], fz[:, g, 0:S - 2], c0, fc[:, g, 2:S],
                                             ALU.mult, ALU.add).then_inc(F.tap, 1)

                def gate(tap, j, par, t):
                    dve.wait_ge(F.tap, tap)
                    dve.wait_ge(F.silu, j)
                    dve.tensor_tensor(fc[:, 1, :], fz[:, 0, :], fc[:, 1, :], ALU.mult).then_inc(F.gated, 1)
                    dve.wait_ge(F.ghi, j)
                    dve.tensor_tensor(g_lo[:, 2 * par + t, :], fc[:, 1, :], g_hi[:, 2 * par + t, :].bitcast(F32),
                                      ALU.subtract).then_inc(F.glo, 1)

                norm_rstd(norm, slot2(1))
                dve.wait_ge(norm.rstd, 1)
                for t in range(4):
                    up(res + t + 1, 0 if t == 0 else t + 1, t % 2)
                    taps(t % 2, t + 1, 2 * t, t)
                    if t % 2:
                        gate(2 * t + 2, t // 2 + 1, 0, t // 2)
                with dve.Fori(0, (NBLK - 1) // 2) as i:
                    for par in range(2):
                        for t in range(4):
                            n = 4 + 12 * par + t
                            u = 4 + 4 * par + t
                            up(i * 24 + (res + n + 1), n + 1, t % 2)
                            taps(t % 2, i * 8 + (u + 1), i * 16 + 2 * u, i * 8 + u)
                            if t % 2:
                                gate(i * 16 + (2 * u + 2), i * 4 + (u // 2 + 1), 1 - par, t // 2)
                        for m in range(KT):
                            n = 4 + 12 * par + 4 + m
                            dve.wait_ge(s_proj, i * 24 + (res + n + 1))
                            dve.tensor_tensor(x[:, m, :], x[:, m, :], slot2(n + 1), ALU.add).then_inc(F.free, 1)
                base = 4 + 12 * (NBLK - 1)
                for m in range(KT):
                    dve.wait_ge(s_proj, res + base + m + 1)
                    dve.tensor_tensor(x[:, m, :], x[:, m, :], slot2(base + m + 1), ALU.add).then_inc(F.free, 1)
                    if m:
                        if not last:
                            act_low(nxt, m - 1)
                        accumulate(nxt, m - 1)
                if not last:
                    act_low(nxt, KT - 1)
                accumulate(nxt, KT - 1)

            ffn(f0, 0, R_F0, norms[1], norms[2], False)

            norm_rstd(norms[2], slot2(3))
            dve.wait_ge(C.rn, 1)
            dve.tensor_copy(tiny[:, 20:28], ps[:, 7, 0:8]).then_inc(C.rnf, 1)
            dve.wait_ge(s_cmx, 16 * 2)
            dve.tensor_tensor(wst[:], wst[:], cst[:, None, C_TRIL:C_TRIL + P].to_broadcast([P, KT, P]), ALU.mult).then_inc(C.ws, 1)
            dve.wait_ge(C.vsq, 16)
            sums = tiny[:, 28:44]
            v8, y8, t8 = tiny[:, 44:52], tiny[:, 52:60], tiny[:, 0:8]
            dve.tensor_tensor(v8, sums[:, 0:8], sums[:, 8:16], ALU.add).then_inc(C.t, 1)
            dve.wait_ge(C.t, 1)
            dve.tensor_scalar(v8, v8, 1.0 / D, EPS, ALU.mult, ALU.add).then_inc(C.t, 1)
            dve.wait_ge(C.ta, 2)
            dve.scalar_tensor_tensor(t8, v8, -0.5, y8, ALU.mult, ALU.mult).then_inc(C.t, 1)
            dve.wait_ge(C.t, 3)
            dve.tensor_tensor(t8, t8, y8, ALU.mult).then_inc(C.t, 1)
            dve.wait_ge(C.t, 4)
            dve.scalar_tensor_tensor(y8, t8, 1.5, y8, ALU.add, ALU.mult).then_inc(C.t, 1)
            dve.wait_ge(C.t, 5)
            for st in range(ST):
                dve.tensor_scalar(vs[:, :, st, :], vs[:, :, st, :], y8[:, st:st + 1], None, ALU.mult).then_inc(C.vn, 1)

            def c_scale(r, m):
                dve.wait_ge(s_proj, R_CU + m + 1)
                if m >= 2:
                    dve.wait_ge(C.gated, m - 1)
                dve.tensor_tensor(cz[:, m % 2, :], slot2(r), rstd[:], ALU.mult).then_inc(C.free, 1)

            def c_gate(m):
                dve.wait_ge(C.u, m + 1)
                t = vs[:, m, :, :].rearrange("p a b -> p (a b)")
                dve.tensor_tensor(t, t, cz[:, m % 2, :], ALU.mult).then_inc(C.gated, 1)

            c_scale(0, 0)
            c_scale(1, 1)
            for g in range(KT):
                r = 2 + g
                dve.wait_ge(C.ready, g + 1)
                dve.scalar_tensor_tensor(vs[:, g, :, :], slot2(r).rearrange("p (a b) -> p a b", b=P),
                                         gain[:, G_SGU + g:G_SGU + g + 1],
                                         bspb[:, None, g * P:(g + 1) * P].to_broadcast([P, ST, P]),
                                         ALU.mult, ALU.add).then_inc(C.free, 1)
            dve.wait_ge(C.free, 10)
            c_gate(0)
            c_gate(1)
            for m in range(2, KT):
                c_scale(8 + m, m)
                c_gate(m)

            residual(WOC, R_WOC, norms[3], False)
            ffn(f1, 1, R_F1, norms[3], norms[4], True)
            norm_rstd(norms[4], slot2(0))
            dve.wait_ge(norms[4].rstd, 1)
            for k in range(KT):
                dve.scalar_tensor_tensor(x[:, k, :], x[:, k, :], gain[:, G_FIN + k:G_FIN + k + 1], rstd[:], ALU.mult,
                                         ALU.mult).then_inc(s_fin, 1)

        @block.scalar
        def _(act):
            def guess(norm):
                act.wait_ge(norm.var, 1)
                act.activation(rstd[:], sq[:, 0, :], ACT.Ln).then_inc(norm.ln, 1)
                act.wait_ge(norm.ln, 1)
                act.activation(rstd[:], rstd[:], ACT.Exp, scale=-0.5).then_inc(norm.exp, 1)

            def high(norm, k):
                act.activation(act_hi[:, k, :], x[:, k, :], ACT.Copy, scale=gain[:, norm.col + k:norm.col + k + 1]
                               ).then_inc(norm.hi, 1)

            def square(norm, k):
                if k >= 2:
                    act.wait_ge(norm.acc, k - 1)
                act.activation(sq[:, k % 2, :], x[:, k, :], ACT.Square).then_inc(norm.sq, 1)

            act.wait_ge(s_cst, 16 * 3)
            for k in range(KT):
                act.wait_ge(s_x[k], 16)
                high(norms[0], k)
                square(norms[0], k)
            guess(norms[0])

            act.wait_ge(s_rope_v, 10)
            act.activation(ropeS[:], r_a[:], ACT.Sin).then_inc(s_rope_a, 1)
            act.activation(r_r[:], r_a[:], ACT.Sin, scale=0.5).then_inc(s_rope_a, 1)

            with act.Fori(0, NBP) as i:
                act.wait_ge(B.free, i * 15 + 4)
                act.activation(b_e[:], b_e[:], ACT.Exp).then_inc(B.e, 1)
                act.wait_ge(B.e, i * 6 + 1)
                act.activation(b_e[:], b_e[:], ACT.Ln, bias=1.0).then_inc(B.e, 1)
                act.wait_ge(B.dec, i * 6 + 1)
                act.activation(b_e[:], b_e[:], ACT.Exp).then_inc(B.e, 1)
                act.wait_ge(B.dec, i * 6 + 3)
                act.activation(b_v[:], b_e[:], ACT.Exp).then_inc(B.e, 1)
                act.wait_ge(B.e, i * 6 + 4)
                act.activation(b_e[:], b_e[:], ACT.Exp, scale=-1.0).then_inc(B.e, 1)
                act.activation(b_cum[:], b_cum[:], ACT.Exp).then_inc(B.e, 1)
                for h in range(2):
                    act.wait_ge(B.free, i * 15 + (11 + h))
                    act.activation(b_r[:, h, :], b_r[:, h, :], ACT.Silu).then_inc(B.silu, 1)
                for h in range(2):
                    act.wait_ge(B.free, i * 15 + (15 + h))
                    if h == 1:
                        act.wait_ge(B.ready, i * 15 + 14)
                    act.activation(b_v[:], (b_k if h == 0 else b_q)[:], ACT.Square).then_inc(B.osq, 1)
                    act.wait_ge(B.o, i * 14 + (2 + 6 * h + 1))
                    act.activation(b_kd[:], b_e[:], ACT.Ln).then_inc(B.osq, 1)
                    act.wait_ge(B.osq, i * 6 + (3 * h + 2))
                    act.activation(b_kd[:], b_kd[:], ACT.Exp, scale=-0.5).then_inc(B.osq, 1)

            def take_vn(hp, h):
                act.wait_ge(A.vt, 2 * hp + h + 1)
                if hp >= 2:
                    act.wait_ge(A.pv, 16 * (hp - 1))
                act.activation(a_vn[hp % 2][:, 4 * h:4 * h + 4, :].rearrange("p a b -> p (a b)"), ps[:, h, :], ACT.Copy
                               ).then_inc(A.vn, 1)

            def exp(U):
                keys = (unit(U)[1] + 1) * P
                act.wait_ge(A.max, U + 1)
                if U >= 4:
                    act.wait_ge(A.rl, U - 3)
                act.activation(a_s[:, U % 3, 0:keys], a_s[:, U % 3, 0:keys], ACT.Exp, scale=-1.0,
                               bias=tiny[:, 8 + U % 4:9 + U % 4], accum_out=tiny[:, 12 + U % 4:13 + U % 4]
                               ).then_inc(A.e, 1)

            def take(U, gi):
                n = min(4, unit(U)[1] + 1 - 4 * gi)
                act.wait_ge(A.pt, groups_before(U) + gi + 1)
                if U >= 2:
                    act.wait_ge(A.pv, U - 1)
                act.activation(a_pt[:, U % 2, 4 * gi * P:(4 * gi + n) * P], ps[:, 6, 0:n * P], ACT.Copy).then_inc(A.ptf, 1)

            def split_high(O, k):
                src = oT[:, k, :] if O is WO else vs[:, k, :, :].rearrange("p a b -> p (a b)")
                act.activation(act_hi[:, k, :], src, ACT.Copy).then_inc(O.hi, 1)

            take_vn(0, 0)
            take_vn(0, 1)
            exp(0)
            exp(1)
            for U in range(UNITS):
                hp, u = U // 16, U % 16
                take(U, 0)
                if U + 2 < UNITS:
                    exp(U + 2)
                if len(groups(unit(U)[1])) == 2:
                    take(U, 1)
                if hp < NHP - 1:
                    for h in range(2):
                        if part_step(T0 + h) == u:
                            take_vn(hp + 1, h)
                elif 1 <= u < 8:
                    if u == 1:
                        act.wait_ge(s_proj, R_WO)
                        act.wait_ge(B.o, 14 * NBP)
                    if u == 7:
                        act.wait_ge(A.of, 24)
                    split_high(WO, WO_ORDER[u - 1])
                if U == UNITS - 8:
                    act.wait_ge(A.pv, 16 * (NHP - 1))
                    act.wait_ge(A.q, 2 * NHP)
                    for k in range(5):
                        act.dma_start(x[:, k, :], xT[k]).then_inc(s_x[k], 16)
            act.wait_ge(A.pt, 24 * NHP)
            for k in range(5, KT):
                act.dma_start(x[:, k, :], xT[k]).then_inc(s_x[k], 16)
            act.wait_ge(A.of, UNITS // 2)
            split_high(WO, NHP - 1)

            def residual(O, res, norm):
                for m in range(KT - 1):
                    act.wait_ge(O.added, m + 1)
                    square(norm, m)
                act.wait_ge(s_proj, res + KT)
                high(norm, 0)
                high(norm, 1)
                act.wait_ge(O.added, KT)
                square(norm, KT - 1)
                for k in range(2, KT):
                    high(norm, k)

            residual(WO, R_WO, norms[1])

            def ffn(F, layer, norm, nxt, last):
                def start(g, n, tile_w, tile_b, cu_free):
                    act.wait_ge(F.free, n)
                    if cu_free is not None:
                        act.wait_ge(F.glo, cu_free)
                    act.activation(fc[:, g, :], fz[:, g, :], ACT.Identity, scale=tile_w, bias=tile_b).then_inc(F.cid, 1)

                def silu(tap):
                    act.wait_ge(F.tap, tap)
                    act.activation(fz[:, 0, :], fc[:, 0, :], ACT.Silu).then_inc(F.silu, 1)

                def g_high(j, par, t):
                    act.wait_ge(F.gated, j)
                    act.activation(g_hi[:, 2 * par + t, :], fc[:, 1, :], ACT.Copy).then_inc(F.ghi, 1)

                guess(norm)
                for t in range(4):
                    start(t % 2, t + 1, cw[:, layer, t, 2:3], cw[:, layer, t, 3:4], 1 if t == 3 else None)
                    if t % 2 == 0:
                        silu(2 * t + 2)
                    else:
                        g_high(t // 2 + 1, 0, t // 2)
                with act.Fori(0, (NBLK - 1) // 2) as i:
                    for par in range(2):
                        for t in range(4):
                            n = 4 + 12 * par + t
                            u = 4 + 4 * par + t
                            tile = i * 8 + u
                            start(t % 2, i * 24 + (n + 1),
                                  cw[:, layer, bass.ds(tile, 1), 2:3].rearrange("p a b -> p (a b)"),
                                  cw[:, layer, bass.ds(tile, 1), 3:4].rearrange("p a b -> p (a b)"),
                                  i * 4 + u // 2 if t % 2 else None)
                            if t % 2 == 0:
                                silu(i * 16 + (2 * u + 2))
                            else:
                                g_high(i * 4 + (u // 2 + 1), 1 - par, t // 2)
                base = 4 + 12 * (NBLK - 1)
                for m in range(KT):
                    act.wait_ge(F.free, base + m + 1)
                    if not last:
                        high(nxt, m)
                    square(nxt, m)

            ffn(f0, 0, norms[1], norms[2], False)

            guess(norms[2])
            act.wait_ge(C.rnf, 1)
            for n in range(16):
                half, st = n // 8, n % 8
                act.wait_ge(s_proj, R_V + n + 1)
                vv = vs[:, 4 * half:4 * half + 4, st, :]
                act.activation(vv, ps[:, n % 6, :].rearrange("p (a b) -> p a b", b=P), ACT.Gelu_apprx_tanh,
                               scale=tiny[:, 20 + st:21 + st]).then_inc(C.vf, 1)
                act.wait_ge(C.vf, n + 1)
                act.activation(sq[:, 0, 0:HALF].rearrange("p (a b) -> p a b", b=P), vv, ACT.Square,
                               accum_out=tiny[:, 28 + n:29 + n]).then_inc(C.vsq, 1)
            act.wait_ge(C.t, 2)
            act.activation(tiny[:, 52:60], tiny[:, 44:52], ACT.Ln).then_inc(C.ta, 1)
            act.wait_ge(C.ta, 1)
            act.activation(tiny[:, 52:60], tiny[:, 52:60], ACT.Exp, scale=-0.5).then_inc(C.ta, 1)
            for m in range(KT):
                act.wait_ge(C.free, m + 1 if m < 2 else 8 + m + 1)
                act.activation(cz[:, m % 2, :], cz[:, m % 2, :], ACT.Gelu_apprx_tanh).then_inc(C.u, 1)
            for k in range(KT):
                act.wait_ge(C.gated, k + 1)
                if k == 0:
                    act.wait_ge(s_proj, R_WOC)
                split_high(WOC, k)
            residual(WOC, R_WOC, norms[3])
            ffn(f1, 1, norms[3], norms[4], True)
            guess(norms[4])


def kernel(x, positions, norm_mix, norm_ffn, w_in_ab, w_gate_up, b_gate_up, g_out_b, w_out_ab, w_in_c, g_sgu,
           w_spatial, b_spatial, w_out_c, w_up, conv_w, conv_b, w_down, norm_final):
    import concourse.bacc as bacc
    from concourse.bass_utils import run_bass_kernel_spmd

    def tiles(w):
        n = w.shape[1] // P
        return np.ascontiguousarray(w.reshape(KT, P, n, P).transpose(2, 1, 0, 3)).reshape(n, P, KT * P)

    def cols(v):
        return v.reshape(-1, P).T

    x, w_in_ab, w_in_c = np.asarray(x), np.asarray(w_in_ab)[0], np.asarray(w_in_c)[0]
    w_up, conv_w, conv_b = np.asarray(w_up), np.asarray(conv_w), np.asarray(conv_b)
    norm_mix, norm_ffn = np.asarray(norm_mix), np.asarray(norm_ffn)
    c, logmul = constant_arrays()
    gains = np.concatenate([cols(norm_mix[0]), cols(norm_mix[1]), cols(norm_ffn[0]), cols(norm_ffn[1]),
                            cols(np.asarray(norm_final)), cols(np.asarray(g_sgu)), cols(np.asarray(g_out_b))], axis=1)
    up = w_up.reshape(2, KT, P, 2, FT, P).transpose(0, 4, 3, 2, 1, 5).reshape(2, 2 * FT, P, KT * P)
    taps = np.concatenate([conv_w, conv_b[:, None]], axis=1)
    taps = taps.reshape(2, 4, 2, FT, P).transpose(4, 0, 3, 2, 1).reshape(P, 2, 2 * FT, 4)
    wv = w_in_c[:, D:].reshape(4, 2, P, 2, HALF).transpose(3, 0, 2, 1, 4).reshape(8, P, 2 * HALF)
    arrays = {
        "xT": x[0].T.reshape(KT, P, S),
        "pos": np.asarray(positions).reshape(1, S),
        "consts": c,
        "logmul": logmul,
        "gains": gains,
        "wgu": np.asarray(w_gate_up)[0],
        "bgu": np.asarray(b_gate_up).reshape(1, 256),
        "wgl": w_in_ab[:, 3072:].reshape(KT, P, 16).transpose(1, 0, 2).reshape(P, KT * 16),
        "w_in": tiles(w_in_ab[:, :3072]),
        "w_out": tiles(np.asarray(w_out_ab)[0]),
        "w_u": tiles(w_in_c[:, :D]),
        "w_v": wv,
        "w_outc": tiles(np.asarray(w_out_c)[0]),
        "wsT": np.asarray(w_spatial)[0].transpose(2, 0, 1),
        "bsp": np.asarray(b_spatial).reshape(1, KT * P),
        "w_up": up,
        "w_dn": np.asarray(w_down).reshape(2, FT, P, D),
        "conv": taps,
    }
    arrays = {n: np.ascontiguousarray(a) for n, a in arrays.items()}
    nc = bacc.Bacc("TRN2", target_bir_lowering=False, num_devices=1)
    args = [nc.dram_tensor(n, a.shape, mybir.dt.from_np(a.dtype), kind="ExternalInput").ap() for n, a in arrays.items()]
    args.append(nc.dram_tensor("outT", (KT, P, S), F32, kind="ExternalOutput").ap())
    build(nc, *args)
    r = run_bass_kernel_spmd(nc, [arrays], core_ids=[0])
    out = r.results[0]["outT"]
    return np.ascontiguousarray(out.reshape(D, S).T).reshape(1, S, D)
```
